# Optimizing a Trainium2 kernel written in Bass

```python
import math
import jax, jax.numpy as jnp
from jax import lax
import numpy as np

D_MODEL = 1024
BATCH = 1
SEQ = 512
DEPTH = 2

CHUNK = 64
Q_BLOCK = 128
EPS = 1e-6

GLA_HEADS = 4
GLA_DK = 64
GLA_DV = 128
GLA_RANK = 16
GLA_TAU = 16.0
DSA_HEADS = 4
DSA_HD = 128
IDX_HEADS = 8
IDX_HD = 64
TOPK_MAX = 256
DIFF_HEADS = 4
DIFF_HD = 64

BR_W = 512
N_BRANCH = 3

SIZES = [
    GLA_HEADS * GLA_DK, GLA_HEADS * GLA_DK, GLA_HEADS * GLA_DV, GLA_RANK, BR_W,
    DSA_HEADS * DSA_HD, DSA_HEADS * DSA_HD, DSA_HEADS * DSA_HD,
    IDX_HEADS * IDX_HD, IDX_HD, IDX_HEADS, BR_W,
    DIFF_HEADS * 2 * DIFF_HD, DIFF_HEADS * 2 * DIFF_HD, DIFF_HEADS * 2 * DIFF_HD, BR_W,
    N_BRANCH * D_MODEL,
]
N_IN = int(sum(SIZES))
SPLIT_AT = [int(s) for s in np.cumsum(SIZES)[:-1]]


F32 = jnp.float32

def _rms(x, g=None):
    xf = x.astype(F32)
    y = xf * lax.rsqrt(jnp.mean(xf * xf, axis=-1, keepdims=True) + EPS)
    if g is not None:
        y = y * g.astype(F32)
    return y.astype(x.dtype)

def _chunk_visible(start, n_q, n_k):
    pos_q = start + jnp.arange(n_q)
    vis_end = (pos_q // CHUNK + 1) * CHUNK
    return jnp.arange(n_k)[None, :] < vis_end[:, None]

def _to_blocks(a, nb):
    return a.reshape((a.shape[0], nb, Q_BLOCK) + a.shape[2:]).swapaxes(0, 1)

def _gla(q, k, v, a_lr, wa2, ba, norm_g):
    B, T, _ = q.shape
    nc = T // CHUNK
    shp = (B, nc, CHUNK, GLA_HEADS)
    q = q.astype(F32).reshape(shp + (GLA_DK,)) * GLA_DK ** -0.5
    k = k.astype(F32).reshape(shp + (GLA_DK,))
    v = v.astype(F32).reshape(shp + (GLA_DV,))
    log_a = jax.nn.log_sigmoid((a_lr @ wa2 + ba).astype(F32)) / GLA_TAU
    log_a = log_a.reshape(shp + (GLA_DK,))
    cum = jnp.cumsum(log_a, axis=2)
    total = cum[:, :, -1]
    k_dec = k * jnp.exp(total[:, :, None] - cum)
    u = jnp.einsum('bnchk,bnchv->nbhkv', k_dec, v)
    decay = jnp.exp(total).transpose(1, 0, 2, 3)

    def step(S, inp):
        a, uc = inp
        S = a[..., None] * S + uc
        return S, S

    S0 = jnp.zeros((B, GLA_HEADS, GLA_DK, GLA_DV), F32)
    _, states = lax.scan(step, S0, (decay, u))
    o = jnp.einsum('bnchk,nbhkv->bnchv', q, states)
    o = _rms(o, norm_g)
    return o.reshape(B, T, GLA_HEADS * GLA_DV)

def _dsa(q, k, v, iq, ik, iw, qn_g, kn_g):
    B, T, _ = q.shape
    nb = T // Q_BLOCK
    topk = min(TOPK_MAX, T // 4)
    q = _rms(q.reshape(B, T, DSA_HEADS, DSA_HD), qn_g)
    k = _rms(k.reshape(B, T, DSA_HEADS, DSA_HD), kn_g)
    v = v.reshape(B, T, DSA_HEADS, DSA_HD)
    iq = iq.reshape(B, T, IDX_HEADS, IDX_HD)
    iw = iw.astype(F32) * IDX_HEADS ** -0.5
    starts = jnp.arange(nb) * Q_BLOCK

    def one(inp):
        qb, iqb, iwb, start = inp
        allowed = _chunk_visible(start, Q_BLOCK, T)
        dots = jnp.einsum('bqhd,bsd->bqhs', iqb, ik, preferred_element_type=F32) * IDX_HD ** -0.5
        score = jnp.einsum('bqhs,bqh->bqs', jax.nn.relu(dots), iwb)
        score = jnp.where(allowed[None], score, -jnp.inf)
        top_val, top_idx = lax.top_k(score, topk)
        valid = jnp.isfinite(top_val)
        k_sel = jax.vmap(lambda kk, ii: kk[ii])(k, top_idx)
        v_sel = jax.vmap(lambda vv, ii: vv[ii])(v, top_idx)
        logits = jnp.einsum('bqhd,bqshd->bhqs', qb, k_sel, preferred_element_type=F32) * DSA_HD ** -0.5
        logits = jnp.where(valid[:, None], logits, -jnp.inf)
        p = jax.nn.softmax(logits, axis=-1).astype(v.dtype)
        return jnp.einsum('bhqs,bqshd->bqhd', p, v_sel)

    out = lax.map(one, (_to_blocks(q, nb), _to_blocks(iq, nb), _to_blocks(iw, nb), starts))
    return out.swapaxes(0, 1).reshape(B, T, DSA_HEADS * DSA_HD)

def _diff(q, k, v, qn_g, kn_g, lq1, lk1, lq2, lk2, lambda_init):
    B, T, _ = q.shape
    nb = T // Q_BLOCK
    q = _rms(q.reshape(B, T, DIFF_HEADS, 2, DIFF_HD), qn_g)
    k = _rms(k.reshape(B, T, DIFF_HEADS, 2, DIFF_HD), kn_g)
    v = v.reshape(B, T, DIFF_HEADS, 2 * DIFF_HD)
    lam = (jnp.exp(jnp.sum(lq1.astype(F32) * lk1.astype(F32)))
           - jnp.exp(jnp.sum(lq2.astype(F32) * lk2.astype(F32))) + lambda_init)
    starts = jnp.arange(nb) * Q_BLOCK

    def one(inp):
        qb, start = inp
        allowed = _chunk_visible(start, Q_BLOCK, T)
        logits = jnp.einsum('bqhcd,bshcd->bhcqs', qb, k, preferred_element_type=F32) * DIFF_HD ** -0.5
        logits = jnp.where(allowed, logits, -jnp.inf)
        p = jax.nn.softmax(logits, axis=-1)
        attn = (p[:, :, 0] - lam * p[:, :, 1]).astype(v.dtype)
        return jnp.einsum('bhqs,bshd->bqhd', attn, v)

    out = lax.map(one, (_to_blocks(q, nb), starts)).swapaxes(0, 1)
    out = _rms(out) * (1.0 - lambda_init)
    return out.reshape(B, T, DIFF_HEADS * 2 * DIFF_HD)

def first_inputs(seed: int = 0) -> dict:
    key = jax.random.key(seed)
    ks = jax.random.split(key, 16)
    nrm = jax.random.normal
    L = DEPTH
    return {
        "x": nrm(ks[0], (BATCH, SEQ, D_MODEL), F32),
        "norm_g": 1.0 + 0.02 * nrm(ks[1], (L, D_MODEL), F32),
        "w_in": nrm(ks[2], (L, D_MODEL, N_IN), F32) * D_MODEL ** -0.5,
        "gla_wa2": nrm(ks[3], (L, GLA_RANK, GLA_HEADS * GLA_DK), F32) * GLA_RANK ** -0.5,
        "gla_ba": 1.0 + 0.1 * nrm(ks[4], (L, GLA_HEADS * GLA_DK), F32),
        "gla_norm_g": 1.0 + 0.02 * nrm(ks[5], (L, GLA_DV), F32),
        "dsa_qn_g": 1.0 + 0.02 * nrm(ks[6], (L, DSA_HD), F32),
        "dsa_kn_g": 1.0 + 0.02 * nrm(ks[7], (L, DSA_HD), F32),
        "diff_qn_g": 1.0 + 0.02 * nrm(ks[8], (L, DIFF_HD), F32),
        "diff_kn_g": 1.0 + 0.02 * nrm(ks[9], (L, DIFF_HD), F32),
        "diff_lq1": 0.1 * nrm(ks[10], (L, DIFF_HD), F32),
        "diff_lk1": 0.1 * nrm(ks[11], (L, DIFF_HD), F32),
        "diff_lq2": 0.1 * nrm(ks[12], (L, DIFF_HD), F32),
        "diff_lk2": 0.1 * nrm(ks[13], (L, DIFF_HD), F32),
        "w_br": nrm(ks[14], (L, N_BRANCH, BR_W, D_MODEL), F32) * BR_W ** -0.5,
        "w_out": nrm(ks[15], (L, D_MODEL, D_MODEL), F32) * D_MODEL ** -0.5,
    }

def first_block(x, norm_g, w_in, gla_wa2, gla_ba, gla_norm_g, dsa_qn_g, dsa_kn_g, diff_qn_g, diff_kn_g,
              diff_lq1, diff_lk1, diff_lq2, diff_lk2, w_br, w_out):
    B, T, _ = x.shape
    for l in range(DEPTH):
        h = _rms(x, norm_g[l])
        proj = h @ w_in[l]
        (gq, gk, gv, ga, gz, bq, bk, bv, iq, ik, iw, bz,
         cq, ck, cv, cz, gate) = jnp.split(proj, SPLIT_AT, axis=-1)
        lambda_init = 0.8 - 0.6 * math.exp(-0.3 * l)
        y_a = _gla(gq, gk, gv, ga, gla_wa2[l], gla_ba[l], gla_norm_g[l]).astype(x.dtype) * jax.nn.silu(gz)
        y_b = _dsa(bq, bk, bv, iq, ik, iw, dsa_qn_g[l], dsa_kn_g[l]) * jax.nn.silu(bz)
        y_c = _diff(cq, ck, cv, diff_qn_g[l], diff_kn_g[l], diff_lq1[l], diff_lk1[l],
                    diff_lq2[l], diff_lk2[l], lambda_init) * jax.nn.silu(cz)
        g = jax.nn.sigmoid(gate.reshape(B, T, N_BRANCH, D_MODEL))
        merged = (g[:, :, 0] * (y_a @ w_br[l, 0])
                  + g[:, :, 1] * (y_b @ w_br[l, 1])
                  + g[:, :, 2] * (y_c @ w_br[l, 2]))
        x = x + merged @ w_out[l]
    return x


MIX_WIDTH = D_MODEL
POOL_WIDTH = D_MODEL // 2
POOL_WINDOWS = (2, 4, 8, 16)
POOL_GROUPS = len(POOL_WINDOWS)
POOL_GC = POOL_WIDTH // POOL_GROUPS
HEAD_DIM = 64
NSA_HEADS = (MIX_WIDTH - POOL_WIDTH) // HEAD_DIM
KV_GROUPS = 2
HEADS_PER_GROUP = NSA_HEADS // KV_GROUPS
CMP_LEN = 32
CMP_STRIDE = 16
SEL_LEN = 64
SEL_TOPN = 16
WINDOW = 512
D_FF = 4 * D_MODEL
ROPE_THETA = 10000.0
NEG = -1e30
FORCED_SCORE = 1e4

Q_COLS = NSA_HEADS * HEAD_DIM
KV_COLS = KV_GROUPS * HEAD_DIM
GATE_COLS = NSA_HEADS * N_BRANCH
IN_COLS = POOL_WIDTH + Q_COLS + 2 * N_BRANCH * KV_COLS + GATE_COLS


def rms_norm(x, g):
    xf = x.astype(jnp.float32)
    y = xf * lax.rsqrt(jnp.mean(xf * xf, axis=-1, keepdims=True) + EPS)
    return (y * g.astype(jnp.float32)).astype(x.dtype)

def rope(x, pos):
    dk = x.shape[-1]
    half = dk // 2
    inv = ROPE_THETA ** (-jnp.arange(half, dtype=jnp.float32) * 2.0 / dk)
    ang = pos.astype(jnp.float32)[:, None] * inv[None, :]
    shape = (1, pos.shape[0]) + (1,) * (x.ndim - 3) + (half,)
    cos = jnp.cos(ang).reshape(shape)
    sin = jnp.sin(ang).reshape(shape)
    xf = x.astype(jnp.float32)
    x1, x2 = xf[..., :half], xf[..., half:]
    return jnp.concatenate([x1 * cos - x2 * sin, x2 * cos + x1 * sin], axis=-1).astype(x.dtype)

def pool_mixer(u, pool_w, pool_scale):
    B, S, _ = u.shape
    ug = u.reshape(B, S, POOL_GROUPS, POOL_GC).astype(jnp.float32)
    cs = jnp.concatenate([jnp.zeros((B, 1, POOL_GROUPS, POOL_GC), jnp.float32),
                          jnp.cumsum(ug, axis=1)], axis=1)
    t = jnp.arange(S)
    win = jnp.array(POOL_WINDOWS, dtype=jnp.int32)
    lower = jnp.maximum(t[:, None] + 1 - win[None, :], 0)
    count = jnp.minimum(t[:, None] + 1, win[None, :]).astype(jnp.float32)
    gidx = jnp.arange(POOL_GROUPS)[None, :]
    sums = cs[:, 1:] - cs[:, lower, gidx]
    pooled = (sums / count[None, :, :, None] - ug).astype(u.dtype)
    y = jnp.einsum('bsgc,gcd->bsgd', pooled, pool_w)
    return y.reshape(B, S, POOL_WIDTH) * pool_scale

def compress(t, pe, w1, w2, blk):
    B = t.shape[0]
    n_cmp = blk.shape[0]
    tb = t[:, blk] + pe[None, None, :, None, :]
    flat = tb.transpose(0, 1, 3, 2, 4).reshape(B, n_cmp, KV_GROUPS, CMP_LEN * HEAD_DIM)
    return jax.nn.silu(flat @ w1) @ w2

def nsa_mixer(q, k_all, v_all, gates, q_norm, k_norm, cmp_pe, cmp_w1, cmp_w2):
    B, S = q.shape[0], q.shape[1]
    G, Hg, dk = KV_GROUPS, HEADS_PER_GROUP, HEAD_DIM
    scale = 1.0 / math.sqrt(dk)
    pos = jnp.arange(S)

    q = rope(rms_norm(q, q_norm), pos).reshape(B, S, G, Hg, dk)
    k_s = rope(rms_norm(k_all[:, :, 1], k_norm[1]), pos)
    k_w = rope(rms_norm(k_all[:, :, 2], k_norm[2]), pos)
    v_s = v_all[:, :, 1]
    v_w = v_all[:, :, 2]

    n_cmp = (S - CMP_LEN) // CMP_STRIDE + 1
    blk = np.arange(n_cmp)[:, None] * CMP_STRIDE + np.arange(CMP_LEN)[None, :]
    cmp_end = jnp.arange(n_cmp) * CMP_STRIDE + (CMP_LEN - 1)
    k_cmp = compress(k_all[:, :, 0], cmp_pe[0], cmp_w1[0], cmp_w2[0], blk)
    v_cmp = compress(v_all[:, :, 0], cmp_pe[1], cmp_w1[1], cmp_w2[1], blk)
    k_cmp = rope(rms_norm(k_cmp, k_norm[0]), cmp_end)
    s_c = jnp.einsum('bsghd,bngd->bsghn', q, k_cmp).astype(jnp.float32) * scale
    mask_c = (cmp_end[None, :] <= pos[:, None])[None, :, None, None, :]
    p_c = jax.nn.softmax(jnp.where(mask_c, s_c, NEG), axis=-1)
    p_c = jnp.where(mask_c, p_c, 0.0)
    o_cmp = jnp.einsum('bsghn,bngd->bsghd', p_c.astype(v_cmp.dtype), v_cmp)

    n_sel = S // SEL_LEN
    cs0 = np.arange(n_cmp) * CMP_STRIDE
    ss0 = np.arange(n_sel) * SEL_LEN
    ov = np.minimum(cs0[:, None] + CMP_LEN, ss0[None, :] + SEL_LEN) - np.maximum(cs0[:, None], ss0[None, :])
    ov_mat = jnp.asarray(np.clip(ov, 0, None).astype(np.float32) / CMP_LEN)
    imp = jnp.einsum('bsghn,nj->bsgj', p_c, ov_mat)
    blk_id = jnp.arange(n_sel)[None, :]
    cur = (pos // SEL_LEN)[:, None]
    causal = blk_id <= cur
    forced = (blk_id == 0) | (blk_id == cur) | (blk_id == cur - 1)
    imp = jnp.where(causal[None, :, None, :],
                    jnp.where(forced[None, :, None, :], FORCED_SCORE, imp), -1.0)
    topn = min(SEL_TOPN, n_sel)
    vals, sel_idx = lax.top_k(imp, topn)
    sel_valid = vals >= 0.0

    k_sb = k_s.reshape(B, n_sel, SEL_LEN, G, dk).transpose(0, 3, 1, 2, 4)
    v_sb = v_s.reshape(B, n_sel, SEL_LEN, G, dk).transpose(0, 3, 1, 2, 4)
    pad = ((0, 0), (WINDOW, 0), (0, 0), (0, 0))
    k_wp = jnp.pad(k_w, pad)
    v_wp = jnp.pad(v_w, pad)
    bi = jnp.arange(B)[:, None, None, None]
    gi = jnp.arange(G)[None, None, :, None]
    C = Q_BLOCK

    def block_fn(qb):
        start = qb * C
        qc = lax.dynamic_slice_in_dim(q, start, C, axis=1)
        tc = start + jnp.arange(C)
        idx = lax.dynamic_slice_in_dim(sel_idx, start, C, axis=1)
        val = lax.dynamic_slice_in_dim(sel_valid, start, C, axis=1)
        kg = k_sb[bi, gi, idx]
        vg = v_sb[bi, gi, idx]
        s = jnp.einsum('bcghd,bcgnld->bcghnl', qc, kg).astype(jnp.float32) * scale
        kpos = idx[..., None] * SEL_LEN + jnp.arange(SEL_LEN)
        m = (kpos <= tc[None, :, None, None, None]) & val[..., None]
        s = jnp.where(m[:, :, :, None], s, NEG)
        sh = s.shape
        p = jax.nn.softmax(s.reshape(sh[:4] + (sh[4] * sh[5],)), axis=-1).reshape(sh)
        o_s = jnp.einsum('bcghnl,bcgnld->bcghd', p.astype(vg.dtype), vg)
        kw = lax.dynamic_slice_in_dim(k_wp, start, C + WINDOW, axis=1)
        vw = lax.dynamic_slice_in_dim(v_wp, start, C + WINDOW, axis=1)
        kpos_w = start - WINDOW + jnp.arange(C + WINDOW)
        diff = tc[:, None] - kpos_w[None, :]
        mw = ((diff >= 0) & (diff < WINDOW) & (kpos_w[None, :] >= 0))[None, :, None, None, :]
        sw = jnp.einsum('bcghd,bkgd->bcghk', qc, kw).astype(jnp.float32) * scale
        pw = jax.nn.softmax(jnp.where(mw, sw, NEG), axis=-1)
        o_w = jnp.einsum('bcghk,bkgd->bcghd', pw.astype(vw.dtype), vw)
        return o_s, o_w

    o_s, o_w = lax.map(block_fn, jnp.arange(S // C))
    o_s = o_s.transpose(1, 0, 2, 3, 4, 5).reshape(B, S, G, Hg, dk)
    o_w = o_w.transpose(1, 0, 2, 3, 4, 5).reshape(B, S, G, Hg, dk)

    g = jax.nn.sigmoid(gates.astype(jnp.float32)).reshape(B, S, G, Hg, N_BRANCH).astype(q.dtype)
    o = g[..., 0:1] * o_cmp + g[..., 1:2] * o_s + g[..., 2:3] * o_w
    return o.reshape(B, S, NSA_HEADS * dk)

def hybrid_layer(x, mod, norm1, norm2, w_in, pool_w, pool_scale, q_norm, k_norm,
                 cmp_pe, cmp_w1, cmp_w2, w_out, w_ff1, w_ff2):
    B, S, _ = x.shape
    shift1, scale1, gate1, shift2, scale2, gate2 = jnp.split(mod[:, None, :], 6, axis=-1)
    h = rms_norm(x, norm1) * (1.0 + scale1) + shift1
    proj = h @ w_in
    o0 = POOL_WIDTH
    o1 = o0 + Q_COLS
    o2 = o1 + 2 * N_BRANCH * KV_COLS
    u = proj[..., :o0]
    q = proj[..., o0:o1].reshape(B, S, NSA_HEADS, HEAD_DIM)
    kv = proj[..., o1:o2].reshape(B, S, 2, N_BRANCH, KV_GROUPS, HEAD_DIM)
    gates = proj[..., o2:]
    y_pool = pool_mixer(u, pool_w, pool_scale)
    y_nsa = nsa_mixer(q, kv[:, :, 0], kv[:, :, 1], gates, q_norm, k_norm, cmp_pe, cmp_w1, cmp_w2)
    mix = jnp.concatenate([y_pool, y_nsa], axis=-1) @ w_out
    x = x + gate1 * mix
    h2 = rms_norm(x, norm2) * (1.0 + scale2) + shift2
    ff = jnp.square(jax.nn.relu(h2 @ w_ff1)) @ w_ff2
    return x + gate2 * ff

def second_inputs(seed: int = 0) -> dict:
    key = jax.random.key(seed)
    ks = jax.random.split(key, 20)
    f32 = jnp.float32
    L, D = DEPTH, D_MODEL
    nrm = lambda k, shape, s: jax.random.normal(k, shape, f32) * s
    return {
        "x": nrm(ks[0], (BATCH, SEQ, D), 1.0),
        "c": nrm(ks[1], (BATCH, D), 1.0),
        "w_mod": nrm(ks[2], (L, D, 6 * D), 0.5 * D ** -0.5),
        "b_mod": nrm(ks[3], (L, 6 * D), 0.01),
        "norm1": 1.0 + nrm(ks[4], (L, D), 0.05),
        "norm2": 1.0 + nrm(ks[5], (L, D), 0.05),
        "w_in": nrm(ks[6], (L, D, IN_COLS), D ** -0.5),
        "pool_w": nrm(ks[7], (L, POOL_GROUPS, POOL_GC, POOL_GC), POOL_GC ** -0.5),
        "pool_scale": 0.5 + nrm(ks[8], (L, POOL_WIDTH), 0.1),
        "q_norm": 1.0 + nrm(ks[9], (L, HEAD_DIM), 0.05),
        "k_norm": 1.0 + nrm(ks[10], (L, N_BRANCH, HEAD_DIM), 0.05),
        "cmp_pe": nrm(ks[11], (L, 2, CMP_LEN, HEAD_DIM), 0.5),
        "cmp_w1": nrm(ks[12], (L, 2, CMP_LEN * HEAD_DIM, HEAD_DIM), (CMP_LEN * HEAD_DIM) ** -0.5),
        "cmp_w2": nrm(ks[13], (L, 2, HEAD_DIM, HEAD_DIM), HEAD_DIM ** -0.5),
        "w_out": nrm(ks[14], (L, MIX_WIDTH, D), MIX_WIDTH ** -0.5),
        "w_ff1": nrm(ks[15], (L, D, D_FF), D ** -0.5),
        "w_ff2": nrm(ks[16], (L, D_FF, D), D_FF ** -0.5),
    }

def second_block(x, c, w_mod, b_mod, norm1, norm2, w_in, pool_w, pool_scale, q_norm, k_norm,
              cmp_pe, cmp_w1, cmp_w2, w_out, w_ff1, w_ff2):
    c_act = jax.nn.silu(c)
    for l in range(DEPTH):
        mod = c_act @ w_mod[l] + b_mod[l]
        x = hybrid_layer(x, mod, norm1[l], norm2[l], w_in[l], pool_w[l], pool_scale[l],
                         q_norm[l], k_norm[l], cmp_pe[l], cmp_w1[l], cmp_w2[l],
                         w_out[l], w_ff1[l], w_ff2[l])
    return x


def setup_inputs(seed=0):
    out = dict(first_inputs(seed))
    for name, value in second_inputs(seed + 1).items():
        if name != "x":
            out[name + "_2"] = value
    return out


def reference(
    x, norm_g, w_in, gla_wa2, gla_ba, gla_norm_g, dsa_qn_g, dsa_kn_g, diff_qn_g, diff_kn_g,
    diff_lq1, diff_lk1, diff_lq2, diff_lk2, w_br, w_out, c_2, w_mod_2, b_mod_2, norm1_2,
    norm2_2, w_in_2, pool_w_2, pool_scale_2, q_norm_2, k_norm_2, cmp_pe_2, cmp_w1_2, cmp_w2_2,
    w_out_2, w_ff1_2, w_ff2_2,
):
    x = first_block(
        x, norm_g, w_in, gla_wa2, gla_ba, gla_norm_g, dsa_qn_g, dsa_kn_g, diff_qn_g, diff_kn_g,
        diff_lq1, diff_lk1, diff_lq2, diff_lk2, w_br, w_out,
    )
    return second_block(
        x, c_2, w_mod_2, b_mod_2, norm1_2, norm2_2, w_in_2, pool_w_2, pool_scale_2, q_norm_2,
        k_norm_2, cmp_pe_2, cmp_w1_2, cmp_w2_2, w_out_2, w_ff1_2, w_ff2_2,
    )


_drawn_inputs = setup_inputs


def setup_inputs(seed=0):
    import zlib

    import numpy as np

    out = dict(_drawn_inputs(seed))
    spreads = {}
    factors = {'gla_norm_g': 5.658,
     'dsa_qn_g': 8.0,
     'dsa_kn_g': 8.0,
     'diff_qn_g': 6.488,
     'diff_kn_g': 6.386,
     'diff_lq1': 3.253,
     'diff_lk1': 4.669,
     'b_mod_2': 3.077,
     'norm1_2': 7.665,
     'q_norm_2': 8.0,
     'k_norm_2': 8.0}
    for name, (base, spread) in spreads.items():
        noise = np.random.default_rng([zlib.crc32(name.encode()), seed]).standard_normal(out[name].shape)
        drawn = base * np.exp(spread * noise) if base else spread * noise
        out[name] = __import__('jax').numpy.asarray(drawn.astype(out[name].dtype))
    for name, factor in factors.items():
        out[name] = (out[name] * factor).astype(out[name].dtype)
    return out
```

```python
import numpy as np
from contextlib import ExitStack

import concourse.bass as bass
from concourse import mybir

ALU = mybir.AluOpType
ACT = mybir.ActivationFunctionType
F32 = mybir.dt.float32
F32R = mybir.dt.float32r
BF16 = mybir.dt.bfloat16
I32 = mybir.dt.int32
AX = mybir.AxisListType.X

P = 128
DEPTH = 2
T = 512
TILES = T // P
D = 1024
KC = D // P
CHUNK = 64
EPS = 1e-6
NEG = -(2.0 ** 100)
TAKEN = -3.0e38
UNSEEN = -1.0e38

C_GQ, C_GK, C_GV, C_GA, C_GZ = 0, 256, 512, 1024, 1040
C_BQ, C_BK, C_BV, C_IQ, C_IK, C_IW, C_BZ = 1552, 2064, 2576, 3088, 3600, 3664, 3672
C_CQ, C_CK, C_CV, C_CZ, C_GATE = 4184, 4696, 5208, 5720, 6232
GLA_RANK, GLA_DK, GLA_TAU, IDX_HEADS, TOPK = 16, 64, 16.0, 8, 128
E_U, E_Q, E_K, E_V = 0, 512, 1024, 1408
N_V = 408
N_CMP, CMP_LEN, CMP_STRIDE = 31, 32, 16
FF_GROUPS = 8
RAW, SPLIT = 3, 5
WIDTH = [P * (t + 1) for t in range(TILES)]
AT = [sum(WIDTH[:t]) for t in range(TILES)]
SCRATCH = 4
MOD_STEPS = 96
MOD_FIRST = 122

COLS = {}


def _cols():
    n = 0
    for l in range(DEPTH):
        for name, k in (("norm_g", 8), ("dsa_q", 1), ("dsa_k", 1), ("diff_q", 1), ("diff_k", 1),
                        ("norm1", 8), ("norm2", 8), ("pool_scale", 4)):
            COLS[name, l] = n
            n += k
    COLS["c"] = n
    return n + 8


N_COLS = _cols()


def unit(name, l, block, col, n, slices, rows=D, w="w_in", row0=0, act="h"):
    quarters, chunks = (1, KC) if name == "small" else (rows // 256, 2)
    return dict(name=name, l=l, block=block, col=col, n=n, slices=slices, quarters=quarters, chunks=chunks,
                w=w, row0=row0, act=act)


def tok(n=512, c0=0):
    return [("tok", t, c0, n) for t in range(TILES)]


def feat(blocks=4, c0=0):
    return [("feat", b, c0 + b * P, P) for b in range(blocks)]


def halves():
    return [(f"feat{half}", b, b * P, P) for half in range(2) for b in range(4)]


def make_timeline(blocks=(1, 2), layers=DEPTH):
    line, units = [], []

    def sweeps(u):
        units.append(u)
        i = len(units) - 1
        return [("sweep", i, p, q) for p in range(len(u["slices"]) // 2) for q in range(u["quarters"])]

    def weave(main, fill):
        n, m, k = len(main), len(fill), 0
        for i, steps in enumerate(main):
            line.extend(steps)
            upto = (i + 1) * m // n
            line.extend(fill[k:upto])
            k = upto

    def norm_head(stage, first, then=[]):
        early = [[("stats", stage, 0)], [("stats", stage, 1)], [("turn", stage, 0)], [("turn", stage, 1)]]
        last = line[-2:] if line else []
        if last and all(x[0] == "sweep" for x in last):
            del line[-2:]
            line.extend([last[0]] + early[0] + [last[1]] + early[1] + [("stats", stage, 2)] + early[2] + early[3] + [("stats", stage, 3)])
        else:
            line.extend(early[0] + early[1] + [("columns",)] + early[2] + early[3] + [("stats", stage, 2), ("stats", stage, 3)])
            then = [("constants",)] + then
        line.extend(first[0:1] + [("turn", stage, 2)] + first[1:2] + [("turn", stage, 3)] + first[2:4] + then + first[4:])

    if 1 in blocks:
        for l in range(layers):
            U = lambda name, col, n, slices, **k: sweeps(unit(name, l, 1, col, n, slices, **k))
            norm_head(("n", l), U("bq", C_BQ, 512, tok()))
            line.append(("vectors", l))
            line.extend(U("iq", C_IQ, 512, feat()))
            line.extend(U("small", C_GA, 88, tok(88)))
            line.append(("rstd", l, "bq"))
            line.extend([("small_turn", l, t) for t in range(TILES)])
            idx = [[("index", l, t, h)] for t in range(TILES) for h in range(IDX_HEADS)]
            weave(idx, U("bk", C_BK, 512, tok()))
            line.append(("rstd", l, "bk"))
            weave([[], []] + [[("key_turn", l, "bk", t)] for t in range(TILES)], U("bv", C_BV, 512, tok()))
            top = [[("topk", l, t, r)] for t in range(1, TILES) for r in range(TOPK // 8)]
            gqk = U("gqk", C_GQ, 512, feat(2) + tok(256, 256))
            weave(top, gqk + U("gv", C_GV, 512, tok()))
            gla = [[("decay1", l, t) for t in range(TILES)] + [("decay2", l)], [], []]
            gla += [[("decay3", l, t) for t in range(TILES)], [], []]
            gla += [[("state", l, t)] for t in range(TILES)]
            weave(gla, U("gz", C_GZ, 512, tok()))
            out = lambda t: [("gla_out", l, t), ("y_tok", l, "a", t)]
            turn = lambda t: [("y_turn", l, "a", t)]
            weave([[], out(0), out(1), turn(0), out(2), turn(1), out(3), turn(2), [], turn(3)], U("bz", C_BZ, 512, tok()))

            def branch(b):
                out = []
                for c in range(2):
                    out += U(f"gate{b}{c}", C_GATE + b * D + c * 512, 512, tok())
                    out += U(f"br{b}{c}", c * 512, 512, tok(), rows=512, w=f"w_br{b}", act="y")
                return out

            line.extend(branch(0))
            items = [(t, h) for t in range(TILES) for h in range(4)]

            def attention(kind, parts):
                main = []
                last = len(items) - 1
                look = lambda n: [("logits", l, kind, *items[n], c) for c in range(parts)] if n <= last else []
                main.append(look(0) + (look(1) if parts == 1 else []))
                for n in range(last + 2):
                    step = []
                    if n <= last:
                        step.append(("prob", l, kind, *items[n]))
                        step.extend(look(n + (2 if parts == 1 else 1)))
                    if n >= 1:
                        step.append(("value", l, kind, *items[n - 1]))
                        if items[n - 1][1] == 3:
                            step.append(("y_tok", l, kind, items[n - 1][0]))
                            if kind == "b":
                                step.append(("y_turn", l, kind, items[n - 1][0]))
                    main.append(step)
                return main

            weave(attention("b", 1), U("cq", C_CQ, 512, tok()) + U("ck", C_CK, 512, tok()))
            line.append(("rstd", l, "cq"))
            line.append(("rstd", l, "ck"))
            weave([[], [], []] + [[("key_turn", l, "ck", t)] for t in range(TILES)], U("cv", C_CV, 512, tok()))
            line.extend(U("cz", C_CZ, 512, tok()))
            weave(attention("c", 2), branch(1))
            line.extend([("y_turn", l, "c", t) for t in range(TILES)])
            line.extend(branch(2))
            out = U("out0", 0, 512, tok(), w="w_out", act="h2") + U("out1", 512, 512, tok(), w="w_out", act="h2")
            line.extend([("merge_turn", l, 0), ("merge_turn", l, 1)] + out[0:1] + [("merge_turn", l, 2)]
                        + out[1:2] + [("merge_turn", l, 3)] + out[2:])
    if 2 in blocks:
        for l in range(layers):
            U = lambda name, col, n, slices, **k: sweeps(unit(name, l, 2, col, n, slices, **k))
            gains = ("gains", l)
            tail = [line.pop() for _ in range(2)][::-1] if line and line[-1][0] == "sweep" else []
            line.append(gains)
            line.extend(tail)
            norm_head(("a", l), U("ek", E_K, 384, tok(384), w="w_in_2", act=("a", l)), [("layer", l)])
            line.append(("rstd", l, "ek"))
            ev = U("ev", E_V, N_V, tok(N_V), w="w_in_2", act=("a", l))
            weave([[], [], [], []] + [[("k_rope", l, t)] for t in range(TILES)], ev)
            line.extend([("cmp_turn", l, t) for t in range(TILES)])
            line.extend([("cmp_in", l, 0), ("cmp_in", l, 1)])
            cmp = [[("cmp_hidden", l, 0)], [("cmp_hidden", l, 1)], [("cmp_key", l)], [("cmp_value", l)], [("cmp_key_turn", l)]]
            weave(cmp, U("eu", E_U, 512, feat(), w="w_in_2", act=("a", l)))
            eq = U("eq", E_Q, 512, tok(), w="w_in_2", act=("a", l))
            line.extend(eq)
            line.append(("rstd", l, "eq"))
            line.append(("gate_row", l, 0))
            line.append(("q_rope", l, 0))
            items = [(t, h) for t in range(TILES) for h in range(8)]
            look = lambda n: ([("cmp_logits", l, items[n][0])] if n < len(items) and items[n][1] == 0 else []) + \
                ([("pair_logits", l, *items[n])] if n < len(items) else [])
            line.extend(look(0) + look(1))
            for n in range(len(items) + 1):
                if n < len(items):
                    t, h = items[n]
                    line.append(("pair_prob", l, t, h))
                    if h == 0:
                        line.append(("cmp_turn2", l, t))
                    if h == 2 and t + 1 < TILES:
                        line.append(("q_rope", l, t + 1))
                    if h == 4:
                        line.append(("pool", l, t))
                    line.extend(look(n + 2))
                if n >= 1:
                    line.append(("pair_value", l, *items[n - 1]))
                    if items[n - 1][1] == 7:
                        line.extend([("o_turn", l, items[n - 1][0])])
            line.extend(U("mix0", 0, 512, tok(), w="w_out_2", act="mix") + U("mix1", 512, 512, tok(), w="w_out_2", act="mix"))
            ff1 = lambda g: U(f"fu{g}", 512 * g, 512, feat() if g else halves(), w="w_ff1_2", act=("f", l))
            ff2 = lambda g: (U(f"fd{g}0", 0, 512, tok(), rows=512, row0=512 * g, w="w_ff2_2", act="ff")
                             + U(f"fd{g}1", 512, 512, tok(), rows=512, row0=512 * g, w="w_ff2_2", act="ff"))
            norm_head(("f", l), ff1(0))
            line.append(("gate_row", l, 1))
            for g in range(1, FF_GROUPS):
                line.extend(ff1(g))
                line.extend(ff2(g - 1))
            line.extend(ff2(FF_GROUPS - 1))

    if 2 in blocks:
        where = {}
        for n, step in enumerate(line):
            beside_head = any(x[0] in ("stats", "turn") for x in line[n:n + 5])
            if step[0] == "sweep" and not beside_head:
                u = units[step[1]]
                if u["name"][:2] in ("iq", "sm", "bz", "cv", "cz", "ou", "fd") or u["name"][:2] == "fu" and u["name"] != "fu0" or u["name"][:5] in ("gate0", "gate2") \
                        or u["name"][:3] in ("br0", "br2"):
                    where.setdefault((u["block"], u["l"] if u["block"] == 2 else 0), []).append(n)
        after = {}
        one, two = where.get((1, 0), []), where.get((2, 0), [])
        for m in range(layers * MOD_STEPS):
            n = one[m * len(one) // MOD_FIRST] if m < MOD_FIRST else \
                two[(m - MOD_FIRST) * len(two) // (layers * MOD_STEPS - MOD_FIRST)]
            after.setdefault(n, []).append(m)
        old, line = line, []
        for n, step in enumerate([None] + old):
            if step == ("gains", layers - 1):
                line.append(("mod_sum", layers * MOD_STEPS // 4 - 1))
            if n:
                line.append(step)
            for m in after.get(n - 1, []):
                if m % 4 == 2 and m >= 4:
                    line.append(("mod_sum", m // 4 - 1))
                line.append(("mod", m))

    late, out = [], []
    for step in line:
        out.append(step)
        if step[0] == "sweep":
            i, p, q = step[1:]
            if late:
                out.extend(late.pop(0))
            u = units[i]
            if u["name"] in ("bq", "cq") and q == u["quarters"] - 1:
                late.append([("q_turn", u["l"], u["name"][0], 2 * p + k) for k in range(2)])
    return out, units




class Ledger:

    def __init__(self, known=None):
        self.count, self.events, self.known = {}, {}, known
        self.sems, self.banks, self.last = {}, {}, {}

    def mark(self, sem, *keys, by=1):
        self.sems[sem.name] = sem
        self.count[sem.name] = self.count.get(sem.name, 0) + by
        for key in keys:
            self.note(key, sem)
        return by

    def note(self, key, sem):
        assert key not in self.events, key
        self.events[key] = (sem.name, self.count[sem.name])

    def now(self, sem):
        return self.count[sem.name]

    def at(self, *key):
        if self.known is None:
            return 1
        return self.known.events[key if len(key) > 1 else key[0]][1]

    def place(self, *key):
        if self.known is None:
            return self.any, 1
        name, value = self.known.events[key if len(key) > 1 else key[0]]
        return self.by_name[name], value


BANK_RINGS = {"proj": ((0,), (1,), (2,), (3,)), "aux": ((4,), (5,), (6,)), "out": ((7,),),
              "pair": ((0, 1), (2, 3), (4, 5)), "aux6": ((6,),)}


def build(nc, a, out, known=None, blocks=(1, 2), layers=DEPTH):
    line, units = make_timeline(blocks, layers)
    start = []
    stream = []
    for u in units:
        start.append(len(stream))
        stream += [(u, q) for q in range(u["quarters"])]
    G = len(stream)
    L = Ledger(known)
    bank_of = known.banks if known else L.banks

    scr_slot, scr_prev, n, holder = {}, {}, 0, {}
    for step in line:
        keys = []
        if step[0] == "sweep":
            _, i, p, q = step
            u = units[i]
            if q == u["quarters"] - 1:
                kind = u["name"]
                if kind in ("bq", "bk", "cq", "ck", "bz", "cz", "gz", "ek", "eq") or kind[:4] in ("gate", "mix0", "mix1") \
                        or kind[:2] == "fu" or kind[:3] == f"fd{FF_GROUPS - 1}":
                    keys = [("scr", i, 2 * p), ("scr", i, 2 * p + 1)]
        elif step[0] == "turn":
            keys = [("scr", step, 0), ("scr", step, 1)]
        elif step[0] == "index" or (step[0] == "y_tok" and step[2] != "c"):
            keys = [("scr", step)]
        elif step[0] in ("k_rope", "q_rope", "cmp_key", "o_turn"):
            keys = [("scr", step)]
        elif step[0] == "pool":
            keys = [("scr", step, 0), ("scr", step, 1)]
        for key in keys:
            scr_slot[key] = n % SCRATCH
            scr_prev[key] = holder.get(n % SCRATCH)
            holder[n % SCRATCH] = key
            n += 1

    seq_of, p_user, len_P, n = {}, {}, {"b": 2, "c": 4}, {}
    for step in line:
        if step[0] == "logits":
            _, l, m, t, h, c = step
            k = n.get((l, m), 0)
            seq_of[step] = k
            p_user[m, l, k] = ("prob", l, m, t, h)
            n[l, m] = k + 1
    slot_of = {p_user[s[2], s[1], k]: k % len_P[s[2]] for s, k in seq_of.items() if s[5] == 0}

    def y_free(step):
        _, l, m, t = step
        if m == "c":
            return [("turned", ("key_turn", l, "ck", TILES - 1))]
        prev = scr_prev["scr", step]
        return [] if prev is None else [("free", prev)]

    def y_at(l, m, t):
        return ybuf[:, t] if m == "c" else scr[:, scr_slot["scr", ("y_tok", l, m, t)]]

    
    with ExitStack() as ctx:
        def sb(name, shape, dt=F32):
            return ctx.enter_context(nc.sbuf_tensor(name, shape, dt))

        def semaphore(name):
            return ctx.enter_context(nc.semaphore(name))

        product, act_high, act_result = semaphore("product"), semaphore("act_high"), semaphore("act_result")
        dve_result, pool_low = semaphore("dve_result"), semaphore("pool_low")
        const_loaded, x_loaded, old_x_loaded = semaphore("const_loaded"), semaphore("x_loaded"), semaphore("old_x_loaded")
        late_loaded = semaphore("late_loaded")
        vec_loaded, cmp_loaded, rates_loaded = semaphore("vec_loaded"), semaphore("cmp_loaded"), semaphore("rates_loaded")
        mod_loaded, raw_loaded = semaphore("mod_loaded"), [semaphore(f"raw_loaded{i}") for i in range(RAW)]
        cmp_w_loaded = semaphore("cmp_w_loaded")
        x_saved, stored = semaphore("x_saved"), semaphore("stored")
        L.any = product
        L.by_name = {sem.name: sem for sem in (product, act_high, act_result, dve_result, pool_low, x_loaded, *raw_loaded)}
        mark, note, at, place, now = L.mark, L.note, L.at, L.place, L.now

        xm = sb("xm", [P, TILES, D])
        hTh, hTl = sb("hTh", [P, KC, T], F32R), sb("hTl", [P, KC, T], F32R)
        yTh, yTl = sb("yTh", [P, 4, T], F32R), sb("yTl", [P, 4, T], F32R)
        raw = sb("raw", [P, RAW, 2, 512])
        wh, wl = sb("wh", [P, SPLIT, 2, 512], F32R), sb("wl", [P, SPLIT, 2, 512], F32R)
        scr = sb("scr", [P, SCRATCH, 512])
        tokr = sb("tokr", [P, 2, 512])
        modw, macc = sb("modw", [P, 2, 256]), sb("macc", [P, 2, 256])
        modT = sb("modT", [P, DEPTH, 48])
        gain = sb("gain", [P, 2, KC])
        cact = sb("cact", [P, 16])
        peT = sb("peT", [P, 64])
        gts = sb("gts", [P, TILES, 24])
        w2s = sb("w2s", [64, 2, 64])
        csoft = sb("csoft", [P, 4, 8])
        with nc.sbuf_tensor("arena", [P, 64 * 256], F32) as arena:
            pass
        f2h, f2l = sb("f2h", [P, 4, T], F32R), sb("f2l", [P, 4, T], F32R)
        arena2 = sb("arena2", [P, 48 * 256])
        cf = sb("cf", [P, 452])
        cb = sb("cb", [P, 128 + 128 + 128 + 128], BF16)
        maskb = sb("maskb", [P, AT[-1] + WIDTH[-1]], BF16)
        colT = sb("colT", [P, N_COLS])
        wab = sb("wab", [17, 256])
        glag = sb("glag", [P, DEPTH, P])
        lam = sb("lam", [P, 8])
        stat = sb("stat", [P, 8, 32])
        nsm = sb("nsm", [P, 4, 32])
        dec = sb("dec", [P, 2, 8])
        top8 = sb("top8", [P, 8])
        soft = sb("soft", [P, 8, 4])
        soft2 = sb("soft2", [P, 8, 8])
        ps = ctx.enter_context(nc.psum_tensor("ps", [P, 8, 512], F32))

        ident, sufm, ind, ones_col = cf[:, 0:128], cf[:, 128:256], cf[:, 256:258], cf[:, 258:259]
        cmprot, edge = cf[:, 259:387], cf[:, 387:387 + 64].rearrange("p (g n) -> p g n", g=4)
        seen = cf[:, 451:452]
        identb, chunkmask, causal = cb[:, 0:128], cb[:, 128:256], cb[:, 256:384]
        cmpmask = cb[:, 384:512].rearrange("p (t n) -> p t n", t=TILES)

        def region(kb, *shape, of=None):
            n = int(np.prod(shape))
            v = (arena if of is None else of)[:, kb * 256:kb * 256 + n]
            names = "abcd"[:len(shape)]
            if len(shape) > 1:
                v = v.rearrange(f"p ({' '.join(names)}) -> p {' '.join(names)}",
                                **{m: s for m, s in zip(names[1:], shape[1:])})
            return v

        qT = {"b": region(0, 4, T), "c": region(32, 4, T)}
        kT = {"b": region(8, 4, T), "c": region(40, 4, T)}
        v_ = {"b": region(16, 4, T), "c": region(0, 4, T)}
        z_ = {"b": region(24, 4, T), "c": region(8, 4, T), "a": region(48, 4, T)}
        PR = {"b": region(48, 2, 512), "c": region(16, 4, 512)}
        PT = {"b": region(52, 2, 512), "c": region(24, 2, 512)}
        ktok = region(56, 4, 512)
        ybuf = region(56, 4, 512)
        xn = region(48, 2, D)
        iqT, ikT = region(32, 4, T), region(29, T)
        smtok, gaT = region(24, 4, 152), region(27, T)
        score = region(40, AT[-1] + WIDTH[-1])
        gqT, gk, gv = region(56, 2, T), region(60, 4, 256), region(32, 4, 512)
        loga, mn = region(40, 4, 256), region(44, 4, 256)
        S = region(40, 2, 8, 128)
        lqk = region(16, 2 * DEPTH * 2, 64)
        cb32 = region(4, 512)
        rows, rows2, rows3 = region(20, 128), region(21, 128), region(22, 128)
        kcd, chid = region(63, 256), region(62, 2, 64)
        kT4, cT, cd, ktk = region(0, 4, T), region(8, 4, T), region(16, 4, 512), region(24, 4, 384)
        rot, qtk, qT8 = region(30, 4, 128), region(32, 4, 512), region(40, 4, T)
        cw, cX = region(32, 2, 16, 64), region(40, 2, 16, 2, 31)
        uT, vt = region(48, 4, T), region(56, 4, 256)
        V4, cS, PTc = region(60, 2, 256), region(62, 256), region(63, 2, P)
        grow, poolw = region(8, D), region(12, 4, P)
        small4 = region(14, 512)
        silk, silv, kcT = small4[:, 0:64], small4[:, 64:320], small4[:, 320:384]
        PP, PPT = region(16, 2, 2, 512), region(24, 2, 2, 512)
        ffacc, grow2 = region(0, TILES, D, of=arena2), region(16, D, of=arena2)
        hgain = glag[:, :, :].rearrange("p l (j n) -> p (l j) n", j=2)
        F = [(yTh, yTl), (f2h, f2l)]
        SS = {"ek": 4, "eq": 5, "bq": 0, "bk": 1, "cq": 2, "ck": 3}

        def q_scale(m, t, h, c):
            n = 4 * t + h if m == "b" else 8 * t + 2 * h + c
            return stat[:, SS[m + "q"], n:n + 1]

        def piece(buffer, slot, u):
            v = buffer[:, slot].rearrange("p c n -> p (c n)")
            return v.rearrange("p (c n) -> p c n", c=u["chunks"])[:, :, 0:u["n"]]

        def col(name, l, k=0, n=1):
            c = COLS[name, l] + k if name != "c" else COLS["c"] + k
            return colT[:, c:c + n]

        def y_parts(step):
            _, l, m, t = step
            y = y_at(l, m, t)
            if m != "a":
                return [(y, ps[:, bank_of.get(("value", l, m, t), 0)], z_[m][:, t])]
            heads = lambda v, odd: v.rearrange("p (n o d) -> p n o d", n=2, o=2)[:, :, odd]
            return [(heads(y, odd), ps[:, bank_of.get((("gla_out", l, t), odd), 0), 0:256].rearrange("p (n d) -> p n d", n=2),
                     heads(z_[m][:, t], odd)) for odd in range(2)]

        w_src = {"w_in_2": lambda u: a["w_in_2"][u["l"]], "w_out_2": lambda u: a["w_out_2"][u["l"]],
                 "w_ff1_2": lambda u: a["w_ff1_2"][u["l"]], "w_ff2_2": lambda u: a["w_ff2_2"][u["l"]],
                 "w_in": lambda u: a["w_in"][u["l"]], "w_out": lambda u: a["w_out"][u["l"]],
                 "w_br0": lambda u: a["w_br"][u["l"], 0], "w_br1": lambda u: a["w_br"][u["l"], 1],
                 "w_br2": lambda u: a["w_br"][u["l"], 2]}

        block = ctx.enter_context(nc.Block())

        @block.sync
        def _(sp):

            def load_weights(g):
                u, q = stream[g]
                if g >= RAW:
                    sp.wait_ge(pool_low, at("low", g - RAW))
                slot = g % RAW
                src = w_src[u["w"]](u)[u["row0"] + 256 * q:u["row0"] + 256 * q + P * u["chunks"], :]
                src = src.rearrange("(c p) n -> p c n", p=P)
                if u["name"] == "small":
                    sp.dma_start(piece(raw, slot, u)[:, :, 0:16], src[:, :, C_GA:C_GA + 16]).then_inc(raw_loaded[slot], mark(raw_loaded[slot], by=16))
                    sp.dma_start(piece(raw, slot, u)[:, :, 16:88], src[:, :, C_IK:C_IK + 72])\
                        .then_inc(raw_loaded[slot], mark(raw_loaded[slot], ("raw", g), by=16))
                else:
                    sp.dma_start(raw[:, slot, :, 0:u["n"]], src[:, :, u["col"]:u["col"] + u["n"]])\
                        .then_inc(raw_loaded[slot], mark(raw_loaded[slot], ("raw", g), by=16))

            sp.dma_start(cf[:], a["cf"]).then_inc(const_loaded, mark(const_loaded, by=16))
            for t in range(TILES):
                sp.dma_start(xm[:, t], a["x"][0, t * P:(t + 1) * P, :]).then_inc(x_loaded, mark(x_loaded, by=16))
            for (name, l), r in [(k, v) for k, v in COLS.items() if isinstance(k, tuple)]:
                src = {"norm_g": "norm_g", "dsa_q": "dsa_qn_g", "dsa_k": "dsa_kn_g", "diff_q": "diff_qn_g",
                       "diff_k": "diff_kn_g", "norm1": "norm1_2", "norm2": "norm2_2",
                       "pool_scale": "pool_scale_2"}[name]
                if name.startswith("diff"):
                    for half in range(2):
                        sp.dma_start(rows[r:r + 1, half * 64:half * 64 + 64], a[src][l:l + 1, :])\
                            .then_inc(const_loaded, mark(const_loaded, by=16))
                else:
                    v = a[src][l].rearrange("(k p) -> k p", p=P)
                    sp.dma_start(rows[r:r + v.shape[0], :], v).then_inc(const_loaded, mark(const_loaded, by=16))
            r = COLS["c"]
            sp.dma_start(rows[r:r + 8, :], a["c_2"][0].rearrange("(k p) -> k p", p=P))\
                .then_inc(const_loaded, mark(const_loaded, by=16))
            note("consts", const_loaded)
            for t in range(TILES):
                note(("x", ("n", 0), t), x_loaded)
            for t in range(TILES):
                if 1 not in blocks:
                    note(("x", ("a", 0), t), x_loaded)
            def load_mod(m):
                l, piece, pairs = m // MOD_STEPS, m % MOD_STEPS // 4, m % 4
                c = slice(256 * piece, 256 * piece + 256)
                if m > 0:
                    sp.wait_ge(dve_result, at("mod", m - 1))
                src = a["w_mod_2"][l, 256 * pairs:256 * pairs + 256, c].rearrange("(c p) n -> p c n", p=P)
                sp.dma_start(modw[:], src).then_inc(mod_loaded, mark(mod_loaded, ("modw", m), by=16))

            issued = min(RAW, G)
            for g in range(issued):
                load_weights(g)
            for step in line:
                if step[0] == "sweep":
                    _, i, p, q = step
                    while issued <= min(start[i] + q + SPLIT + RAW if p == len(units[i]["slices"]) // 2 - 1
                                        else start[i] + SPLIT + RAW - 1, G - 1):
                        load_weights(issued)
                        issued += 1
                elif step[0] == "stats" and step[1][0] == "n" and step[1][1] > 0:
                    l, t = step[1][1], step[2]
                    sp.wait_ge(*place("x", ("n", l), t))
                    sp.dma_start(a["x_kept"][l, t], xm[:, t]).then_inc(x_saved, mark(x_saved, ("saved", l, t), by=16))
                elif step[0] == "constants":
                    sp.dma_start(cb32, a["cb"]).then_inc(late_loaded, mark(late_loaded, by=16))
                    for l in range(DEPTH):
                        sp.dma_start(rows3[48 * l:48 * l + 48, :], a["b_mod_2"][l].rearrange("(k p) -> k p", p=P))\
                            .then_inc(late_loaded, mark(late_loaded, by=16))
                        sp.dma_start(glag[:, l], a["gla_norm_g"][l].partition_broadcast(P)).then_inc(late_loaded, mark(late_loaded, by=16))
                        for j, name in enumerate(("diff_lq1", "diff_lk1", "diff_lq2", "diff_lk2")):
                            sp.dma_start(lqk[:, 4 * l + j], a[name][l].partition_broadcast(P))\
                                .then_inc(late_loaded, mark(late_loaded, by=16))
                    for l in range(DEPTH):
                        for kv in range(2):
                            j = 16 * (2 * l + kv)
                            for hf in range(2):
                                sp.dma_start(rows2[j:j + 16, hf * 64:hf * 64 + 64],
                                             a["cmp_pe_2"][l, kv, hf * 16:hf * 16 + 16, :]).then_inc(late_loaded, mark(late_loaded, by=16))
                    note("late consts", late_loaded)
                    if 2 in blocks:
                        load_mod(0)
                elif step[0] == "vectors":
                    l = step[1]
                    if l > 0:
                        sp.wait_ge(product, at("rates", l - 1, TILES - 1))
                    sp.dma_start(wab[0:16], a["gla_wa2"][l]).then_inc(rates_loaded, mark(rates_loaded, by=16))
                    sp.dma_start(wab[16:17], a["gla_ba"][l:l + 1, :]).then_inc(rates_loaded, mark(rates_loaded, ("wab", l), by=16))
                elif step[0] == "mod":
                    if step[1] + 1 < MOD_STEPS * layers:
                        load_mod(step[1] + 1)
                elif step[0] == "layer":
                    l = step[1]
                    if l > 0:
                        sp.wait_ge(product, at("arena_done", l - 1))
                        sp.wait_ge(*place("x", ("a", l), TILES - 1))
                    elif 1 in blocks:
                        sp.wait_ge(product, at("merged_turned", layers - 1, 0))
                    vl = lambda dst, src: sp.dma_start(dst, src).then_inc(vec_loaded, mark(vec_loaded, by=16))
                    vl(rot, a["rot"].rearrange("(t p) n -> p t n", p=P))
                    vl(hgain[:, 0], a["q_norm_2"][l].partition_broadcast(P))
                    for j in range(3):
                        vl(hgain[:, 1 + j], a["k_norm_2"][l, (1, 2, 0)[j]].partition_broadcast(P))
                    note(("rope_loaded", l), vec_loaded)
                    vl = lambda dst, src: sp.dma_start(dst, src).then_inc(cmp_w_loaded, mark(cmp_w_loaded, by=16))
                    for kv in range(2):
                        for hf in range(2):
                            vl(cw[64 * hf:64 * hf + 64, kv],
                               a["cmp_w1_2"][l, kv, 1024 * hf:1024 * hf + 1024, :].rearrange("(s d) j -> d s j", d=64))
                        vl(w2s[:, kv], a["cmp_w2_2"][l, kv])
                    note(("layer_loaded", l), cmp_w_loaded)
                elif step[0] == "cmp_hidden" and step[2] == 1:
                    l = step[1]
                    sp.wait_ge(dve_result, at("cX", l, 0))
                    sp.wait_ge(dve_result, at("cX", l, 1))
                    sp.dma_start(poolw, a["pool_w_2"][l].rearrange("g c d -> c g d")).then_inc(cmp_loaded, mark(cmp_loaded, ("poolw", l), by=16))
                elif step[0] == "merge_turn":
                    _, l, t = step
                    sp.wait_ge(product, at("merged_turned", l, t))
                    if l == 0:
                        src = a["x"][0, t * P:(t + 1) * P, :]
                    else:
                        for tt in range(TILES):
                            sp.wait_ge(x_saved, at("all_saved", l))
                        src = a["x_kept"][l, t]
                    sp.dma_start(xm[:, t], src).then_inc(old_x_loaded, mark(old_x_loaded, by=16))
                    if t == TILES - 1:
                        for tt in range(TILES):
                            note(("old_x", l, tt), old_x_loaded)
                if step[0] == "stats" and step[1][0] == "n" and step[1][1] > 0 and step[2] == TILES - 1:
                    note(("all_saved", step[1][1]), x_saved)
            for t in range(TILES):
                sp.wait_ge(*place("x", "end", t))
                sp.dma_start(out[0, t * P:(t + 1) * P, :], xm[:, t]).then_inc(stored, mark(stored, by=16))
            sp.wait_ge(stored, now(stored))

        @block.gpsimd
        def _(pool):
            for g in range(G):
                u = stream[g][0]
                pool.wait_ge(act_high, at("high", g))
                pool.tensor_tensor(piece(wl, g % SPLIT, u), piece(raw, g % RAW, u),
                                   piece(wh, g % SPLIT, u).bitcast(F32), ALU.subtract)\
                    .then_inc(pool_low, mark(pool_low, ("low", g)))

        @block.tensor
        def _(pe):
            turn = {}

            def bank(ring, key):
                n = turn.get(ring, 0)
                turn[ring] = n + 1
                b = BANK_RINGS[ring][n % len(BANK_RINGS[ring])]
                for x in b:
                    if x in L.last:
                        pe.wait_ge(*place("free", L.last[x]))
                    L.last[x] = key
                L.banks[key] = b[0]
                return ps[:, b[0]:b[0] + 2] if len(b) == 2 else ps[:, b[0]]

            def turn4(dst, src, n=4):
                for c in range(n):
                    last = pe.transpose(dst[:, c * P:(c + 1) * P], src[:, c * P:(c + 1) * P], ident)
                return last

            def sweep(i, p, q):
                u = units[i]
                g = start[i] + q
                pair = u["slices"][2 * p:2 * p + 2]
                pe.wait_ge(pool_low, at("low", g))
                Ah, Al = (yTh, yTl) if u["act"] == "y" else (hTh, hTl)
                if u["act"] == "ff":
                    Ah, Al = F[int(u["name"][2]) % 2]
                if q == 0:
                    for s in (2 * p, 2 * p + 1):
                        bank("proj", ("ps", i, s))
                for k, (mode, idx, c0, n) in enumerate(pair):
                    s = 2 * p + k
                    o = ps[:, L.banks["ps", i, s]]
                    for t in {"tok": [idx], "feat": range(TILES), "feat0": (0, 1), "feat1": (2, 3)}[mode]:
                        if u["act"] == "h":
                            pe.wait_ge(dve_result, at("h", ("n", u["l"]), t, 1 if u["chunks"] == KC else q // 2))
                        elif u["act"] == "h2":
                            pe.wait_ge(dve_result, at("m", u["l"], t, q // 2))
                        elif u["act"] == "mix":
                            if q < 2:
                                pe.wait_ge(dve_result, at("pooled", u["l"], 2 * q))
                                pe.wait_ge(dve_result, at("pooled", u["l"], 2 * q + 1))
                            else:
                                pe.wait_ge(dve_result, at("mo", u["l"], t))
                        elif u["act"] == "ff":
                            pe.wait_ge(dve_result, at("f", u["l"], int(u["name"][2]), 2 * q))
                            pe.wait_ge(dve_result, at("f", u["l"], int(u["name"][2]), 2 * q + 1))
                        elif isinstance(u["act"], tuple):
                            pe.wait_ge(dve_result, at("h", u["act"], t, q // 2))
                        else:
                            pe.wait_ge(dve_result, at("y", u["l"], "abc"[int(u["name"][2])], t))
                    for c in range(u["chunks"]):
                        x = 2 * q + c
                        for n_pass, (A, W) in enumerate(((Ah, wh), (Ah, wl), (Al, wh))):
                            w = piece(W, g % SPLIT, u)[:, c]
                            if mode == "tok":
                                args = (o[:, 0:n], A[:, x, idx * P:(idx + 1) * P], w[:, c0:c0 + n])
                            elif mode == "feat":
                                args = (o, w[:, c0:c0 + n], A[:, x, :])
                            else:
                                lo = 256 * int(mode[4])
                                args = (o[:, 0:256], w[:, c0:c0 + n], A[:, x, lo:lo + 256])
                            last = pe.matmul(*args, start=(q == 0 and c == 0 and n_pass == 0),
                                             stop=(q == u["quarters"] - 1 and c == u["chunks"] - 1 and n_pass == 2))
                    keys = []
                    if q == u["quarters"] - 1:
                        keys.append(("product", i, s))
                    if p == len(u["slices"]) // 2 - 1 and k == 1:
                        keys.append(("used", g))
                    if keys and u["name"][:2] == "fd" and u["name"][3] == "1" and s == 3 and q == u["quarters"] - 1:
                        keys.append(("ff_read", u["l"], int(u["name"][2])))
                        if u["name"][2] == str(FF_GROUPS - 1):
                            keys.append(("arena_done", u["l"]))
                    if keys:
                        last.then_inc(product, mark(product, *keys))

            pe.wait_ge(const_loaded, at("consts"))
            for step in line:
                kind = step[0]
                if kind == "sweep":
                    sweep(*step[1:])
                elif kind == "columns":
                    b = bank("aux", "cols")
                    pe.transpose(b[:, 0:N_COLS], rows[0:N_COLS, :], ident[0:N_COLS, 0:N_COLS])\
                        .then_inc(product, mark(product, "rows_turned"))
                elif kind == "constants":
                    b = bank("aux", "late cols")
                    pe.wait_ge(late_loaded, at("late consts"))
                    pe.transpose(b[:, 256:352], rows3[0:96, :], ident[0:96, 0:96])
                    pe.transpose(b[:, 128:192], rows2[0:64, :], ident[0:64, 0:64])\
                        .then_inc(product, mark(product, "late_rows_turned"))
                elif kind == "turn":
                    _, stage, t = step
                    pe.wait_ge(dve_result, at("xn", stage, t))
                    for hb in range(2):
                        b = bank("aux", (step, hb))
                        turn4(b, xn[:, t % 2, hb * 512:(hb + 1) * 512]).then_inc(product, mark(product, ("turned", step, hb)))
                elif kind == "q_turn":
                    _, l, m, t = step
                    b = bank("aux", step)
                    pe.wait_ge(act_result, at("tok", l, m, t))
                    turn4(b, tokr[:, t % 2]).then_inc(product, mark(product, ("turned", step)))
                elif kind == "key_turn":
                    _, l, m, t = step
                    b = bank("aux", step)
                    pe.wait_ge(dve_result, at("scaled_key", l, m, t))
                    turn4(b, ktok[:, t]).then_inc(product, mark(product, ("turned", step)))
                elif kind == "small_turn":
                    _, l, t = step
                    b = bank("aux", step)
                    pe.wait_ge(act_result, at("small", l, t))
                    pe.transpose(b[:, 0:P], smtok[:, t, 0:P], ident)
                    pe.transpose(b[0:16, P:2 * P], smtok[:, t, P:P + 16], ident)\
                        .then_inc(product, mark(product, ("turned", step)))
                elif kind == "index":
                    _, l, t, h = step
                    b = bank("aux", step)
                    half = slice(64 * (h % 2), 64 * (h % 2) + 64)
                    for tt in range(t + 1):
                        pe.wait_ge(act_result, at("small_turned", l, tt))
                    pe.wait_ge(act_result, at("iq", l, h // 2))
                    pe.matmul(b[:, 0:WIDTH[t]], iqT[half, h // 2, t * P:(t + 1) * P], ikT[half, 0:WIDTH[t]],
                              start=True, stop=True).then_inc(product, mark(product, ("dots", step)))
                elif kind == "decay1":
                    _, l, t = step
                    b = bank("aux", step)
                    pe.wait_ge(act_result, at("small_turned", l, t))
                    pe.wait_ge(rates_loaded, at("wab", l))
                    pe.matmul(b[:, 0:256], gaT[0:17, t * P:(t + 1) * P], wab[:], start=True, stop=True)\
                        .then_inc(product, mark(product, ("rates", l, t)))
                elif kind == "decay3":
                    _, l, t = step
                    b = bank("aux", step)
                    pe.wait_ge(dve_result, at("loga", l))
                    pe.matmul(b[:, 0:256], sufm, loga[:, t], start=True, stop=True)
                    for pr in range(2):
                        last = pe.matmul(b[:, 256 + 2 * pr:258 + 2 * pr], loga[:, t, pr * P:(pr + 1) * P], ind,
                                         start=True, stop=True)
                    last.then_inc(product, mark(product, ("sums", l, t)))
                elif kind == "state":
                    _, l, t = step
                    pe.wait_ge(dve_result, at("decayed_key", l, t))
                    pe.wait_ge(act_result, at("gv", l, t))
                    for cc in range(2):
                        b = bank("aux", (step, cc))
                        tk = slice(64 * cc, 64 * cc + 64)
                        for pr in range(2):
                            last = pe.matmul(b[:, pr * 256:(pr + 1) * 256], gk[tk, t, pr * P:(pr + 1) * P],
                                             gv[tk, t, pr * 256:(pr + 1) * 256], start=True, stop=True)
                        last.then_inc(product, mark(product, ("update", l, t, cc)))
                elif kind == "gla_out":
                    _, l, t = step
                    pe.wait_ge(dve_result, at("states", l, t))
                    pe.wait_ge(act_result, at("gqT", l, 0))
                    pe.wait_ge(act_result, at("gqT", l, 1))
                    for odd in range(2):
                        b = bank("out" if odd == 0 else "aux", (step, odd))
                        dk = slice(64 * odd, 64 * odd + 64)
                        for cc in range(2):
                            for pr in range(2):
                                lo = t * P + 64 * cc
                                last = pe.matmul(b[64 * cc:64 * cc + 64, pr * P:(pr + 1) * P],
                                                 gqT[dk, pr, lo:lo + 64], S[dk, pr, 2 * t + cc, :],
                                                 start=True, stop=True)
                    last.then_inc(product, mark(product, ("out", l, "a", t)))
                elif kind == "y_turn":
                    _, l, m, t = step
                    b = bank("aux", step)
                    pe.wait_ge(dve_result, at("y_tok", l, m, t))
                    keys = [] if m == "c" else [("free", ("scr", ("y_tok", l, m, t)))]
                    turn4(b, y_at(l, m, t)).then_inc(product, mark(product, ("turned", step), *keys))
                elif kind == "logits":
                    _, l, m, t, h, c = step
                    W = WIDTH[t]
                    b = bank("aux", step)
                    pe.wait_ge(act_result, at("qT", l, m, t))
                    for tt in range(t + 1):
                        pe.wait_ge(act_result, at("kT", l, m, tt))
                    tile = slice(t * P, (t + 1) * P)
                    if m == "b":
                        pe.wait_ge(dve_result, at("mask", l, t))
                        pe.matmul(b[:, 0:W], qT[m][:, h, tile], kT[m][:, h, 0:W], start=True, stop=False)
                        last = pe.matmul(b[:, 0:W], identb, maskb[:, AT[t]:AT[t] + W], start=False, stop=True)
                    else:
                        d = slice(64 * c, 64 * c + 64)
                        pe.matmul(b[:, 0:W], qT[m][d, h, tile], kT[m][d, h, 0:W], start=True, stop=False)
                        last = pe.matmul(b[:, W - P:W], identb, chunkmask, start=False, stop=True)
                    last.then_inc(product, mark(product, ("logits", step)))
                elif kind == "prob":
                    _, l, m, t, h = step
                    b = bank("aux", step)
                    pe.wait_ge(dve_result, at("prob", step))
                    src = PR[m][:, slot_of[step]]
                    turn4(b, src, t + 1).then_inc(product, mark(product, ("turned", step)))
                elif kind == "value":
                    _, l, m, t, h = step
                    n = 4 * t + h
                    if h == 0:
                        bank("out", ("value", l, m, t))
                    b = ps[:, L.banks["value", l, m, t]]
                    pe.wait_ge(*place("PT", l, m, n))
                    for tt in range(t + 1):
                        pe.wait_ge(act_result, at("v", l, m, tt))
                    for j in range(t + 1):
                        last = pe.matmul(b[:, h * P:(h + 1) * P], PT[m][:, n % 2, j * P:(j + 1) * P],
                                         v_[m][:, j, h * P:(h + 1) * P], start=(j == 0), stop=(j == t))
                    last.then_inc(product, mark(product, ("value", l, m, n), *([("out", l, m, t)] if h == 3 else [])))
                elif kind == "mod_sum":
                    b = bank("aux", step)
                    j = step[1]
                    pe.wait_ge(dve_result, at("mod", 4 * j + 3))
                    for c in range(2):
                        last = pe.matmul(b[:, c:c + 1], macc[:, j % 2, c * P:(c + 1) * P], ones_col, start=True, stop=True)
                    last.then_inc(product, mark(product, ("mod_sum", j)))
                elif kind == "k_rope":
                    _, l, t = step
                    b = bank("aux", step)
                    pe.wait_ge(dve_result, at("roped_k", l, t))
                    turn4(b, tokr[:, t % 2]).then_inc(product, mark(product, ("turned", step)))
                elif kind == "q_rope":
                    _, l, t = step
                    b = bank("aux6", step)
                    pe.wait_ge(dve_result, at("roped_q", l, t))
                    turn4(b, tokr[:, t % 2]).then_inc(product, mark(product, ("turned", step)))
                elif kind == "cmp_turn":
                    _, l, t = step
                    b = bank("aux", step)
                    pe.wait_ge(act_result, at("cdk", l, t))
                    pe.wait_ge(act_result, at("cdv", l, t))
                    turn4(b, cd[:, t]).then_inc(product, mark(product, ("turned", step)))
                elif kind == "cmp_hidden":
                    _, l, kv = step
                    b = bank("aux", step)
                    pe.wait_ge(dve_result, at("cX", l, kv))
                    pe.wait_ge(cmp_w_loaded, at("layer_loaded", l))
                    for j in range(16):
                        last = pe.matmul(b[0:64, 0:62], cw[:, kv, j], cX[:, kv, j].rearrange("p g n -> p (g n)"),
                                         start=(j == 0), stop=(j == 15))
                    last.then_inc(product, mark(product, ("hidden", l, kv)))
                elif kind == "cmp_key":
                    _, l = step
                    b = bank("aux", step)
                    pe.wait_ge(dve_result, at("silk", l))
                    for g in range(2):
                        last = pe.matmul(b[0:32, 64 * g:64 * g + 64], silk[0:64, 32 * g:32 * g + 32], w2s[:, 0],
                                         start=True, stop=True)
                    last.then_inc(product, mark(product, ("kcmp", l)))
                elif kind == "cmp_value":
                    _, l = step
                    b = bank("aux", step)
                    pe.wait_ge(dve_result, at("silv", l))
                    for g in range(2):
                        last = pe.matmul(b[:, 64 * g:64 * g + 64], silv[0:64, P * g:P * g + P], w2s[:, 1],
                                         start=True, stop=True)
                    last.then_inc(product, mark(product, ("vcmp", l)))
                elif kind == "cmp_key_turn":
                    _, l = step
                    b = bank("aux", step)
                    pe.wait_ge(dve_result, at("kc_roped", l))
                    for g in range(2):
                        last = pe.transpose(b[:, 32 * g:32 * g + 32], kcd[0:32, P * g:P * g + P], ident[0:32, 0:32])
                    last.then_inc(product, mark(product, ("turned", step)))
                elif kind == "pool":
                    _, l, g = step
                    b = bank("aux6", step)
                    pe.wait_ge(dve_result, at("pooled_in", l, g))
                    pe.wait_ge(cmp_loaded, at("poolw", l))
                    pe.matmul(b, poolw[:, g], scr[:, scr_slot["scr", step, 0]], start=True, stop=True)\
                        .then_inc(product, mark(product, ("pool_out", l, g), ("free", ("scr", step, 0))))
                elif kind == "gate_row":
                    _, l, which = step
                    b = bank("pair", step)
                    pe.wait_ge(dve_result, at("modT", l))
                    for c in range(KC):
                        k = (16, 40)[which] + c
                        last = pe.matmul(b[:, c // 4, (c % 4) * P:(c % 4 + 1) * P],
                                         modT[:, l, k:k + 1].to_broadcast([P, P]), ident, start=True, stop=True)
                    last.then_inc(product, mark(product, ("gate_row", l, which)))
                elif kind == "cmp_logits":
                    _, l, t = step
                    b = bank("pair", step)
                    pe.wait_ge(act_result, at("q8T", l, t))
                    pe.wait_ge(act_result, at("kcT", l))
                    for odd in range(2):
                        d = slice(64 * odd, 64 * odd + 64)
                        pe.matmul(b[:, odd, 0:P], identb, cmpmask[:, t].unsqueeze(1).to_broadcast([P, 4, 32]),
                                  start=True, stop=False)
                        for n in range(4):
                            last = pe.matmul(b[:, odd, 32 * n:32 * n + 32], qT8[d, n, t * P:(t + 1) * P],
                                             kcT[d, 32 * (n // 2):32 * (n // 2) + 32], start=False, stop=(n == 3))
                    last.then_inc(product, mark(product, ("cmp_logits", l, t)))
                elif kind == "pair_logits":
                    _, l, t, h = step
                    W = WIDTH[t]
                    b = bank("pair", step)
                    pe.wait_ge(act_result, at("q8T", l, t))
                    for tt in range(t + 1):
                        pe.wait_ge(act_result, at("k4T", l, tt))
                    d = slice(64 * (h % 2), 64 * (h % 2) + 64)
                    for j in range(2):
                        pe.matmul(b[:, j, 0:W], qT8[d, h // 2, t * P:(t + 1) * P], kT4[d, 2 * j + h // 4, 0:W],
                                  start=True, stop=False)
                        last = pe.matmul(b[:, j, W - P:W], identb, causal, start=False, stop=True)
                    last.then_inc(product, mark(product, ("logits", step)))
                elif kind == "pair_prob":
                    _, l, t, h = step
                    n = 8 * t + h
                    b = bank("pair", step)
                    pe.wait_ge(dve_result, at("prob", step))
                    for j in range(2):
                        last = turn4(b[:, j], PP[:, n % 2, j], t + 1)
                    last.then_inc(product, mark(product, ("turned", step)))
                elif kind == "cmp_turn2":
                    _, l, t = step
                    b = bank("pair", step)
                    pe.wait_ge(dve_result, at("cmp_prob", l, t))
                    for g in range(2):
                        last = pe.transpose(b[:, 0, g * P:(g + 1) * P], cS[:, g * P:(g + 1) * P], ident)
                    last.then_inc(product, mark(product, ("turned", step)))
                elif kind == "pair_value":
                    _, l, t, h = step
                    n = 8 * t + h
                    if h == 0:
                        bank("out", ("o", l, t))
                    b = ps[:, L.banks["o", l, t]]
                    if h == 0:
                        pe.wait_ge(act_result, at("PTc", l, t))
                        pe.wait_ge(act_result, at("V4", l))
                        for g in range(2):
                            pe.matmul(b[:, g * 256:(g + 1) * 256], PTc[:, g], V4[:, g], start=(g == 0), stop=False)
                    pe.wait_ge(*place("PPT", l, n))
                    for tt in range(t + 1):
                        pe.wait_ge(act_result, at("vt", l, tt))
                    for j in range(2):
                        for c in range(t + 1):
                            lo = j * P + 64 * (h // 4)
                            last = pe.matmul(b[:, h * 64:h * 64 + 64], PPT[:, n % 2, j, c * P:(c + 1) * P],
                                             vt[:, c, lo:lo + 64], start=False, stop=(h == 7 and j == 1 and c == t))
                    last.then_inc(product, mark(product, ("value2", l, n), *([("o", l, t)] if h == 7 else [])))
                elif kind == "o_turn":
                    _, l, t = step
                    b = bank("aux6", step)
                    pe.wait_ge(act_result, at("o_tok", l, t))
                    turn4(b, scr[:, scr_slot["scr", step]]).then_inc(product, mark(product, ("turned", step), ("free", ("scr", step))))
                elif kind == "merge_turn":
                    _, l, t = step
                    pe.wait_ge(dve_result, at("merged", l, t))
                    for hb in range(2):
                        b = bank("aux", (step, hb))
                        last = turn4(b, xm[:, t, hb * 512:(hb + 1) * 512])
                        last.then_inc(product, mark(product, ("turned", step, hb), *([("merged_turned", l, t)] if hb else [])))

        @block.scalar
        def _(act):

            def high(g):
                u = stream[g][0]
                act.wait_ge(*place("raw", g))
                if g >= SPLIT:
                    act.wait_ge(product, at("used", g - SPLIT))
                act.activation(piece(wh, g % SPLIT, u), piece(raw, g % RAW, u), ACT.Copy)\
                    .then_inc(act_high, mark(act_high, ("high", g)))

            for g in range(RAW):
                high(g)
            made = [RAW]

            def scratch(key):
                if scr_prev[key] is not None:
                    act.wait_ge(*place("free", scr_prev[key]))
                return scr[:, scr_slot[key]]

            def evacuate(i, s):
                u = units[i]
                l, name = u["l"], u["name"]
                mode, idx, c0, n = u["slices"][s]
                b = ps[:, bank_of.get(("ps", i, s), 0)]
                free = ("free", ("ps", i, s))
                if name[:2] in ("br", "ou", "mi") or (name[:2] == "fd" and name[2] != "0"):
                    return
                act.wait_ge(product, at("product", i, s))
                if name in ("bq", "cq", "bk", "ck"):
                    if name[1] == "q":
                        dst = tokr[:, idx % 2]
                        if idx >= 2:
                            act.wait_ge(product, at("turned", ("q_turn", l, name[0], idx - 2)))
                        elif (name, l) != ("bq", 0):
                            prev = ("cq", l - 1) if name == "bq" else ("bq", l)
                            act.wait_ge(product, at("turned", ("q_turn", prev[1], prev[0][0], idx + 2)))
                        act.activation(dst, b, ACT.Copy).then_inc(act_result, mark(act_result, ("tok", l, name[0], idx)))
                    else:
                        act.activation(ktok[:, idx], b, ACT.Copy).then_inc(act_result, mark(act_result, ("ktok", l, name[0], idx)))
                    key = ("scr", i, s)
                    act.activation(scratch(key), b, ACT.Square).then_inc(act_result, mark(act_result, ("sq", i, s), free))
                elif name in ("bv", "cv"):
                    act.activation(v_[name[0]][:, idx], b, ACT.Copy).then_inc(act_result, mark(act_result, ("v", l, name[0], idx), free))
                elif name in ("bz", "cz", "gz") or name.startswith("gate"):
                    act.activation(scratch(("scr", i, s)), b, ACT.Tanh, scale=0.5)\
                        .then_inc(act_result, mark(act_result, ("tanh", i, s), *([free] if name.startswith("gate") else [])))
                elif name == "iq":
                    act.activation(iqT[:, idx], b, ACT.Copy).then_inc(act_result, mark(act_result, ("iq", l, idx), free))
                elif name == "small":
                    act.activation(smtok[:, idx, 0:P].rearrange("p (r d) -> p r d", r=2),
                                   b[:, 16:80].unsqueeze(1).to_broadcast([P, 2, 64]), ACT.Copy)
                    act.activation(smtok[:, idx, P:P + 16], b[:, 0:16], ACT.Copy)
                    act.activation(smtok[:, idx, P + 16:P + 24], b[:, 80:88], ACT.Copy,
                                   scale=float(np.float32(IDX_HEADS ** -0.5) * np.float32(0.125)))\
                        .then_inc(act_result, mark(act_result, ("small", l, idx), free))
                elif name == "gqk":
                    if mode == "feat":
                        act.activation(gqT[:, idx], b, ACT.Copy, scale=GLA_DK ** -0.5)\
                            .then_inc(act_result, mark(act_result, ("gqT", l, idx), free))
                    else:
                        act.activation(gk[:, idx], b[:, 0:256], ACT.Copy).then_inc(act_result, mark(act_result, ("gk", l, idx), free))
                elif name == "ek":
                    act.activation(cd[:, idx, 0:256].rearrange("p (g r d) -> p g r d", g=2, r=2),
                                   b[:, 0:P].rearrange("p (g d) -> p g d", g=2).unsqueeze(2).to_broadcast([P, 2, 2, 64]),
                                   ACT.Copy).then_inc(act_result, mark(act_result, ("cdk", l, idx)))
                    act.activation(ktk[:, idx, 0:256], b[:, 128:384], ACT.Copy).then_inc(act_result, mark(act_result, ("ktk", l, idx)))
                    act.activation(scratch(("scr", i, s))[:, 0:256], b[:, 128:384], ACT.Square)\
                        .then_inc(act_result, mark(act_result, ("sq", i, s), free))
                elif name == "ev":
                    act.activation(cd[:, idx, 256:512].rearrange("p (g r d) -> p g r d", g=2, r=2),
                                   b[:, 0:P].rearrange("p (g d) -> p g d", g=2).unsqueeze(2).to_broadcast([P, 2, 2, 64]),
                                   ACT.Copy).then_inc(act_result, mark(act_result, ("cdv", l, idx)))
                    act.activation(vt[:, idx], b[:, 128:384], ACT.Copy).then_inc(act_result, mark(act_result, ("vt", l, idx)))
                    act.activation(gts[:, idx], b[:, 384:408], ACT.Tanh, scale=0.5)\
                        .then_inc(act_result, mark(act_result, ("gates_tanh", l, idx), free))
                elif name == "eu":
                    act.activation(uT[:, idx], b, ACT.Copy).then_inc(act_result, mark(act_result, ("uT", l, idx), free))
                elif name == "eq":
                    act.activation(qtk[:, idx], b, ACT.Copy).then_inc(act_result, mark(act_result, ("qtk", l, idx)))
                    act.activation(scratch(("scr", i, s)), b, ACT.Square).then_inc(act_result, mark(act_result, ("sq", i, s), free))
                elif name[:2] == "fu":
                    g = int(name[2])
                    act.wait_ge(dve_result, at("relu2", i, s))
                    if g >= 2:
                        act.wait_ge(product, at("ff_read", l, g - 2))
                    t0, n = (0, T) if mode == "feat" else (256 * int(mode[4]), 256)
                    act.activation(F[g % 2][0][:, idx, t0:t0 + n], scr[:, scr_slot["scr", i, s], 0:n], ACT.Copy)\
                        .then_inc(act_result, mark(act_result, ("fh", i, s)))
                elif name[:2] == "fd":
                    c = int(name[3])
                    act.activation(ffacc[:, idx, c * 512:(c + 1) * 512], b, ACT.Copy)\
                        .then_inc(act_result, mark(act_result, ("ffacc", l, c, idx), free))
                elif name == "gv":
                    act.activation(gv[:, idx], b, ACT.Copy).then_inc(act_result, mark(act_result, ("gv", l, idx), free))
                else:
                    raise ValueError(name)

            while made[0] < SPLIT and 1 in blocks:
                high(made[0])
                made[0] += 1
            for step in line:
                kind = step[0]
                if kind == "sweep":
                    _, i, p, q = step
                    last_pair = p == len(units[i]["slices"]) // 2 - 1
                    while made[0] <= min(start[i] + q + SPLIT if last_pair else start[i] + SPLIT - 1, G - 1):
                        high(made[0])
                        made[0] += 1
                    if q == units[i]["quarters"] - 1:
                        evacuate(i, 2 * p)
                        evacuate(i, 2 * p + 1)
                elif kind == "constants":
                    if 2 in blocks:
                        act.wait_ge(dve_result, at("cols"))
                        act.activation(cact[:, 8:16], col("c", 0, 0, 8), ACT.Tanh, scale=0.5).then_inc(act_result, mark(act_result, "c_tanh"))
                    act.wait_ge(dve_result, at("lambda_sums"))
                    act.activation(lam[:, 4:8], lam[:, 0:4], ACT.Exp).then_inc(act_result, mark(act_result, "lambda_exps"))
                elif kind == "stats":
                    _, stage, t = step
                    act.wait_ge(*place("x", stage, t))
                    if t >= 2:
                        act.wait_ge(product, at("turned", ("turn", stage, t - 2), 1))
                    act.activation(xn[:, t % 2], xm[:, t], ACT.Square, accum_out=stat[:, 7, t:t + 1])\
                        .then_inc(act_result, mark(act_result, ("ss", stage, t)))
                elif kind == "turn":
                    _, stage, t = step
                    for hb in range(2):
                        act.wait_ge(dve_result, at("h32", step, hb))
                        act.activation(hTh[:, 4 * hb:4 * hb + 4, t * P:(t + 1) * P],
                                       scr[:, scr_slot["scr", step, hb]].rearrange("p (c n) -> p c n", c=4), ACT.Copy)\
                            .then_inc(act_result, mark(act_result, ("hh", step, hb)))
                elif kind in ("q_turn", "key_turn"):
                    _, l, m, t = step
                    m = m[0]
                    r = "q" if kind == "q_turn" else "k"
                    dst = (qT if r == "q" else kT)[m][:, :, t * P:(t + 1) * P]
                    name = {"b": "dsa_", "c": "diff_"}[m] + r
                    act.wait_ge(product, at("turned", step))
                    act.wait_ge(dve_result, at("cols"))
                    act.activation(dst, ps[:, bank_of.get(step, 0)].rearrange("p (h n) -> p h n", h=4), ACT.Copy,
                                   scale=col(name, l)).then_inc(act_result, mark(act_result, (r + "T", l, m, t), ("free", step)))
                elif kind == "small_turn":
                    _, l, t = step
                    b = ps[:, bank_of.get(step, 0)]
                    act.wait_ge(product, at("turned", step))
                    act.wait_ge(dve_result, at("ones_row", l))
                    act.activation(ikT[:, t * P:(t + 1) * P], b[:, 0:P], ACT.Copy)
                    act.activation(gaT[0:16, t * P:(t + 1) * P], b[0:16, P:2 * P], ACT.Copy)\
                        .then_inc(act_result, mark(act_result, ("small_turned", l, t), ("free", step)))
                elif kind == "index":
                    _, l, t, h = step
                    act.wait_ge(product, at("dots", step))
                    act.activation(scratch(("scr", step))[:, 0:WIDTH[t]], ps[:, bank_of.get(step, 0), 0:WIDTH[t]], ACT.Relu)\
                        .then_inc(act_result, mark(act_result, ("relu", step), ("free", step)))
                elif kind == "decay1":
                    _, l, t = step
                    act.wait_ge(product, at("rates", l, t))
                    act.wait_ge(dve_result, at("mask", l, TILES - 1))
                    b = ps[:, bank_of.get(step, 0), 0:256]
                    act.activation(loga[:, t], b, ACT.Abs).then_inc(act_result, mark(act_result, ("abs", l, t)))
                    act.wait_ge(act_result, at("abs", l, t))
                    act.activation(loga[:, t], loga[:, t], ACT.Exp, scale=-1.0).then_inc(act_result, mark(act_result, ("expabs", l, t)))
                elif kind == "decay2":
                    _, l = step
                    act.wait_ge(act_result, at("expabs", l, TILES - 1))
                    act.activation(loga[:, :, :], loga[:, :, :], ACT.Ln, bias=1.0).then_inc(act_result, mark(act_result, ("ln", l)))
                elif kind == "decay3":
                    _, l, t = step
                    act.wait_ge(product, at("sums", l, t))
                    act.wait_ge(dve_result, at("loga", l))
                    b = ps[:, bank_of.get(step, 0)]
                    act.activation(mn[:, t], b[:, 0:256], ACT.Exp, scale=1.0 / GLA_TAU)
                    act.activation(dec[:, :, 2 * t:2 * t + 2], b[:, 256:260].rearrange("p (a b) -> p a b", a=2),
                                   ACT.Exp, scale=1.0 / GLA_TAU).then_inc(act_result, mark(act_result, ("decays", l, t), ("free", step)))
                elif kind == "y_tok":
                    _, l, m, t = step
                    if m in ("a", "c"):
                        act.wait_ge(product, at("out", l, m, t))
                        for key in y_free(step):
                            act.wait_ge(*place(key))
                        for y, b, _ in y_parts(step):
                            ins = act.activation(y, b, ACT.Square)
                        ins.then_inc(act_result, mark(act_result, ("osq", step)))
                elif kind == "y_turn":
                    _, l, m, t = step
                    act.wait_ge(product, at("turned", step))
                    act.activation(yTh[:, :, t * P:(t + 1) * P], ps[:, bank_of.get(step, 0)].rearrange("p (c n) -> p c n", c=4),
                                   ACT.Copy).then_inc(act_result, mark(act_result, ("yh", step)))
                elif kind == "logits":
                    _, l, m, t, h, c = step
                    W = WIDTH[t]
                    n = seq_of[step]
                    act.wait_ge(dve_result, at("bias", step))
                    if n >= len_P[m]:
                        act.wait_ge(product, at("turned", p_user[m, l, n - len_P[m]]))
                    s = soft[:, n % 8]
                    act.activation(PR[m][:, n % len_P[m], 0:W], ps[:, bank_of.get(step, 0), 0:W], ACT.Exp,
                                   bias=s[:, 1:2], scale=q_scale(m, t, h, c), accum_out=s[:, 2:3])\
                        .then_inc(act_result, mark(act_result, ("exp", step), ("free", step)))
                elif kind == "prob":
                    _, l, m, t, h = step
                    n = 4 * t + h
                    if n % 2 == 0:
                        act.wait_ge(product, at("turned", step))
                        if n >= 2:
                            act.wait_ge(product, at("value", l, m, n - 2))
                        act.activation(PT[m][:, n % 2, 0:WIDTH[t]], ps[:, bank_of.get(step, 0), 0:WIDTH[t]], ACT.Copy)\
                            .then_inc(act_result, mark(act_result, ("PT", l, m, n), ("free", step)))
                elif kind in ("k_rope", "q_rope"):
                    _, l, t = step
                    dst = (kT4 if kind == "k_rope" else qT8)[:, :, t * P:(t + 1) * P]
                    act.wait_ge(product, at("turned", step))
                    act.activation(dst, ps[:, bank_of.get(step, 0)].rearrange("p (h n) -> p h n", h=4), ACT.Copy)\
                        .then_inc(act_result, mark(act_result, ("k4T" if kind == "k_rope" else "q8T", l, t), ("free", step)))
                elif kind == "cmp_turn":
                    _, l, t = step
                    b = ps[:, bank_of.get(step, 0)].rearrange("p (j n) -> p j n", j=4)
                    act.wait_ge(product, at("turned", step))
                    act.activation(cT[0:64, :, t * P:(t + 1) * P], b[0:64], ACT.Copy)
                    skip = 16 if t == 0 else 0
                    act.activation(cT[64:P, :, t * P - 16 + skip:(t + 1) * P - 16], b[64:P, :, skip:P], ACT.Copy)\
                        .then_inc(act_result, mark(act_result, ("cT", l, t), ("free", step)))
                elif kind == "cmp_hidden":
                    _, l, kv = step
                    act.wait_ge(product, at("hidden", l, kv))
                    act.wait_ge(dve_result, at("sil_cleared", l))
                    act.activation(chid[0:64, kv, 0:62], ps[0:64, bank_of.get(step, 0), 0:62], ACT.Tanh, scale=0.5)\
                        .then_inc(act_result, mark(act_result, ("hidden_tanh", l, kv)))
                elif kind == "cmp_value":
                    _, l = step
                    act.wait_ge(product, at("vcmp", l))
                    act.wait_ge(dve_result, at("V4_cleared", l))
                    b = ps[:, bank_of.get(step, 0), 0:P].rearrange("p (g d) -> p g d", g=2)
                    for n in range(4):
                        r = slice(32 * n, 32 * n + 32)
                        ins = act.activation(V4[r, :, 64 * n:64 * n + 64], b[r], ACT.Copy, scale=0.5)
                    ins.then_inc(act_result, mark(act_result, ("V4", l), ("free", step)))
                elif kind == "cmp_key":
                    _, l = step
                    act.wait_ge(product, at("kcmp", l))
                    act.activation(kcd[0:32, 0:128], ps[0:32, bank_of.get(step, 0), 0:128], ACT.Copy, scale=0.5)\
                        .then_inc(act_result, mark(act_result, ("kc_raw", l), ("free", step)))
                elif kind == "cmp_key_turn":
                    _, l = step
                    act.wait_ge(product, at("turned", step))
                    act.activation(kcT, ps[:, bank_of.get(step, 0), 0:64], ACT.Copy).then_inc(act_result, mark(act_result, ("kcT", l), ("free", step)))
                elif kind == "pool":
                    _, l, g = step
                    act.wait_ge(product, at("pool_out", l, g))
                    act.activation(hTh[:, g], ps[:, bank_of.get(step, 0)], ACT.Copy, scale=col("pool_scale", l, g))\
                        .then_inc(act_result, mark(act_result, ("pool_high", l, g)))
                elif kind == "gate_row":
                    _, l, which = step
                    act.wait_ge(product, at("gate_row", l, which))
                    if which == 0:
                        act.wait_ge(dve_result, at("cX", l, 0))
                        act.wait_ge(dve_result, at("cX", l, 1))
                    b0 = bank_of.get(step, 0)
                    act.activation((grow, grow2)[which].rearrange("p (o n) -> p o n", o=2), ps[:, b0:b0 + 2], ACT.Copy)\
                        .then_inc(act_result, mark(act_result, ("grow", l, which), ("free", step)))
                elif kind == "cmp_logits":
                    _, l, t = step
                    act.wait_ge(dve_result, at("cmp_shifted", l, t))
                    act.activation(cS, cS, ACT.Exp, scale=0.125).then_inc(act_result, mark(act_result, ("cmp_exp", l, t)))
                elif kind == "pair_logits":
                    _, l, t, h = step
                    n, W = 8 * t + h, WIDTH[t]
                    b0 = bank_of.get(step, 0)
                    s = soft2[:, n % 8]
                    act.wait_ge(dve_result, at("bias", step))
                    if n >= 2:
                        act.wait_ge(product, at("turned", ("pair_prob", l, (n - 2) // 8, (n - 2) % 8)))
                    for j in range(2):
                        ins = act.activation(PP[:, n % 2, j, 0:W], ps[:, b0 + j, 0:W], ACT.Exp, bias=s[:, 2 + j:3 + j],
                                             scale=0.125, accum_out=s[:, 4 + j:5 + j])
                    ins.then_inc(act_result, mark(act_result, ("exp", step), ("free", step)))
                elif kind == "pair_prob" and (8 * step[2] + step[3]) % 2 == 0:
                    _, l, t, h = step
                    n, W, b0 = 8 * t + h, WIDTH[t], bank_of.get(step, 0)
                    act.wait_ge(product, at("turned", step))
                    if n >= 2:
                        act.wait_ge(product, at("value2", l, n - 2))
                    act.activation(PPT[:, n % 2, :, 0:W], ps[:, b0:b0 + 2, 0:W], ACT.Copy)\
                        .then_inc(act_result, mark(act_result, ("PPT", l, n), ("free", step)))
                elif kind == "cmp_turn2":
                    _, l, t = step
                    act.wait_ge(product, at("turned", step))
                    if t > 0:
                        act.wait_ge(product, at("value2", l, 8 * t - 8))
                    act.activation(PTc, ps[:, bank_of.get(step, 0), 0:256].rearrange("p (g n) -> p g n", g=2), ACT.Copy)\
                        .then_inc(act_result, mark(act_result, ("PTc", l, t), ("free", step)))
                elif kind == "o_turn":
                    _, l, t = step
                    act.wait_ge(product, at("o", l, t))
                    act.activation(scratch(("scr", step)), ps[:, bank_of.get(("o", l, t), 0)], ACT.Copy)\
                        .then_inc(act_result, mark(act_result, ("o_tok", l, t), ("free", ("o", l, t))))
                    act.wait_ge(product, at("turned", step))
                    act.activation(hTh[:, 4:8, t * P:(t + 1) * P], ps[:, bank_of.get(step, 0)].rearrange("p (c n) -> p c n", c=4),
                                   ACT.Copy).then_inc(act_result, mark(act_result, ("oh", l, t)))
                elif kind == "merge_turn":
                    _, l, t = step
                    for hb in range(2):
                        act.wait_ge(product, at("turned", step, hb))
                        act.activation(hTh[:, 4 * hb:4 * hb + 4, t * P:(t + 1) * P],
                                       ps[:, bank_of.get((step, hb), 0)].rearrange("p (c n) -> p c n", c=4), ACT.Copy, scale=0.5)\
                            .then_inc(act_result, mark(act_result, ("mh", step, hb)))

        @block.vector
        def _(dve):
            def rsqrt(y, v):
                m, n = v.shape[0], v.shape[-1]
                half, tmp = nsm[0:m, 2, 0:n], nsm[0:m, 3, 0:n]
                dve.tensor_scalar(y.bitcast(I32), v.bitcast(I32), 1, None, ALU.logical_shift_right)\
                    .then_inc(dve_result, mark(dve_result))
                dve.wait_ge(dve_result, now(dve_result))
                dve.tensor_scalar(y.bitcast(I32), y.bitcast(I32), -1.0, float(0x5f3759df), ALU.mult, ALU.add)\
                    .then_inc(dve_result, mark(dve_result))
                dve.wait_ge(dve_result, now(dve_result))
                dve.tensor_scalar(half, v, -0.5, None, ALU.mult).then_inc(dve_result, mark(dve_result))
                dve.wait_ge(dve_result, now(dve_result))
                for _ in range(3):
                    dve.tensor_tensor(tmp, y, y, ALU.mult).then_inc(dve_result, mark(dve_result))
                    dve.wait_ge(dve_result, now(dve_result))
                    dve.tensor_tensor(tmp, tmp, half, ALU.mult).then_inc(dve_result, mark(dve_result))
                    dve.wait_ge(dve_result, now(dve_result))
                    dve.scalar_tensor_tensor(y, tmp, 1.5, y, ALU.add, ALU.mult).then_inc(dve_result, mark(dve_result))
                    dve.wait_ge(dve_result, now(dve_result))

            def evacuate(i, s):
                u = units[i]
                l, name = u["l"], u["name"]
                mode, idx, c0, n = u["slices"][s]
                b = ps[:, bank_of.get(("ps", i, s), 0)]
                free = ("free", ("ps", i, s))
                key = ("scr", i, s)
                if name in ("ek", "eq"):
                    nh = 4 if name == "ek" else 8
                    dve.wait_ge(act_result, at("sq", i, s))
                    dve.tensor_reduce(stat[:, SS[name], idx * nh:(idx + 1) * nh],
                                      scr[:, scr_slot[key], 0:64 * nh].rearrange("p (h d) -> p h d", h=nh), AX, ALU.add)\
                        .then_inc(dve_result, mark(dve_result, ("sumsq", l, name, idx), ("free", key)))
                elif name == "ev":
                    dve.wait_ge(act_result, at("gates_tanh", l, idx))
                    dve.tensor_scalar(gts[:, idx], gts[:, idx], 1.0, 0.5, ALU.add, ALU.mult)\
                        .then_inc(dve_result, mark(dve_result, ("gates", l, idx)))
                    dve.wait_ge(dve_result, now(dve_result))
                    if idx == 0:
                        g3 = gts[:, 0].rearrange("p (h b) -> p h b", b=3)[:, :, 0]
                        dve.tensor_scalar(g3, g3, seen, None, ALU.mult).then_inc(dve_result, mark(dve_result))
                        dve.wait_ge(dve_result, now(dve_result))
                elif name[:3] == "mix":
                    c = int(name[3])
                    dst = xm[:, idx, c * 512:(c + 1) * 512]
                    tmp = scr[:, scr_slot[key]]
                    dve.wait_ge(product, at("product", i, s))
                    dve.wait_ge(act_result, at("grow", l, 0))
                    if scr_prev[key] is not None:
                        dve.wait_ge(*place("free", scr_prev[key]))
                    dve.tensor_tensor(tmp, b, grow[:, c * 512:(c + 1) * 512], ALU.mult)\
                        .then_inc(dve_result, mark(dve_result, free))
                    dve.wait_ge(dve_result, now(dve_result))
                    dve.tensor_tensor(dst, dst, tmp, ALU.add)\
                        .then_inc(dve_result, mark(dve_result, ("free", key), *([("x", ("f", l), idx)] if c else [])))
                elif name[:2] == "fu":
                    g = int(name[2])
                    t0, n = (0, T) if mode == "feat" else (256 * int(mode[4]), 256)
                    tmp, b = scr[:, scr_slot[key], 0:n], b[:, 0:n]
                    dve.wait_ge(product, at("product", i, s))
                    if scr_prev[key] is not None:
                        dve.wait_ge(*place("free", scr_prev[key]))
                    dve.tensor_scalar(tmp, b, 0.0, None, ALU.max).then_inc(dve_result, mark(dve_result))
                    dve.wait_ge(dve_result, now(dve_result))
                    dve.tensor_tensor(tmp, b, tmp, ALU.mult).then_inc(dve_result, mark(dve_result, ("relu2", i, s), free))
                    dve.wait_ge(dve_result, now(dve_result))
                    dve.wait_ge(act_result, at("fh", i, s))
                    dve.tensor_tensor(F[g % 2][1][:, idx, t0:t0 + n], tmp, F[g % 2][0][:, idx, t0:t0 + n].bitcast(F32), ALU.subtract)\
                        .then_inc(dve_result, mark(dve_result, ("free", key), *([] if mode == "feat0" else [("f", l, g, idx)])))
                elif name[:2] == "fd":
                    g, c = int(name[2]), int(name[3])
                    acc = ffacc[:, idx, c * 512:(c + 1) * 512]
                    if g == 0:
                        return
                    dve.wait_ge(product, at("product", i, s))
                    dve.wait_ge(act_result, at("ffacc", l, c, idx))
                    if g < FF_GROUPS - 1:
                        dve.tensor_tensor(acc, b, acc, ALU.add).then_inc(dve_result, mark(dve_result, free))
                        dve.wait_ge(dve_result, now(dve_result))
                        return
                    dst = xm[:, idx, c * 512:(c + 1) * 512]
                    tmp = scr[:, scr_slot[key]]
                    dve.wait_ge(act_result, at("grow", l, 1))
                    if scr_prev[key] is not None:
                        dve.wait_ge(*place("free", scr_prev[key]))
                    dve.tensor_tensor(tmp, b, acc, ALU.add).then_inc(dve_result, mark(dve_result, free))
                    dve.wait_ge(dve_result, now(dve_result))
                    dve.tensor_tensor(tmp, tmp, grow2[:, c * 512:(c + 1) * 512], ALU.mult)\
                        .then_inc(dve_result, mark(dve_result))
                    dve.wait_ge(dve_result, now(dve_result))
                    stage = ("a", l + 1) if l + 1 < layers else "end"
                    dve.tensor_tensor(dst, dst, tmp, ALU.add)\
                        .then_inc(dve_result, mark(dve_result, ("free", key), *([("x", stage, idx)] if c else [])))
                elif name in ("bq", "cq", "bk", "ck"):
                    nh = 4 if name[0] == "b" else 8
                    dve.wait_ge(act_result, at("sq", i, s))
                    dve.tensor_reduce(stat[:, SS[name], idx * nh:(idx + 1) * nh],
                                      scr[:, scr_slot[key]].rearrange("p (h d) -> p h d", h=nh), AX, ALU.add)\
                        .then_inc(dve_result, mark(dve_result, ("sumsq", l, name, idx), ("free", key)))
                elif name in ("bz", "cz", "gz"):
                    m = {"bz": "b", "cz": "c", "gz": "a"}[name]
                    dve.wait_ge(act_result, at("tanh", i, s))
                    dve.scalar_tensor_tensor(z_[m][:, idx], scr[:, scr_slot[key]], 1.0, b, ALU.add, ALU.mult)\
                        .then_inc(dve_result, mark(dve_result, ("z", l, m, idx), free, ("free", key)))
                elif name.startswith("br"):
                    c = int(name[3])
                    gate = ("scr", i - 1, s)
                    g = scr[:, scr_slot[gate]]
                    dst = xm[:, idx, c * 512:(c + 1) * 512]
                    dve.wait_ge(product, at("product", i, s))
                    dve.wait_ge(act_result, at("tanh", i - 1, s))
                    fin = [("merged", l, idx)] if name == "br21" else []
                    if name[2] == "0":
                        if l > 0:
                            dve.wait_ge(x_saved, at("all_saved", l))
                        dve.scalar_tensor_tensor(dst, g, 1.0, b, ALU.add, ALU.mult)\
                            .then_inc(dve_result, mark(dve_result, ("free", gate), free, *fin))
                    else:
                        dve.scalar_tensor_tensor(g, g, 1.0, b, ALU.add, ALU.mult)\
                            .then_inc(dve_result, mark(dve_result, free))
                        dve.wait_ge(dve_result, now(dve_result))
                        dve.tensor_tensor(dst, dst, g, ALU.add).then_inc(dve_result, mark(dve_result, ("free", gate), *fin))
                elif name.startswith("out"):
                    c = int(name[3])
                    dst = xm[:, idx, c * 512:(c + 1) * 512]
                    dve.wait_ge(product, at("product", i, s))
                    dve.wait_ge(old_x_loaded, at("old_x", l, idx))
                    stage = ("n", l + 1) if l + 1 < layers else ("a", 0) if 2 in blocks else "end"
                    fin = [("x", stage, idx)] if c == 1 else []
                    dve.tensor_tensor(dst, b, dst, ALU.add).then_inc(dve_result, mark(dve_result, free, *fin))

            def rotate(x, tmp, table, nh, rows=P):
                for half in range(2):
                    sine = table[:, 64 + 32 * half:96 + 32 * half].unsqueeze(1).to_broadcast([rows, nh, 32])
                    dve.tensor_tensor(tmp[:, :, 32 * half:32 * half + 32], x[:, :, 32 - 32 * half:64 - 32 * half],
                                      sine, ALU.mult).then_inc(dve_result, mark(dve_result))
                    dve.wait_ge(dve_result, now(dve_result))
                dve.tensor_tensor(x, x, table[:, 0:64].unsqueeze(1).to_broadcast([rows, nh, 64]), ALU.mult)\
                    .then_inc(dve_result, mark(dve_result))
                dve.wait_ge(dve_result, now(dve_result))

            for step in line:
                kind = step[0]
                if kind == "sweep":
                    _, i, p, q = step
                    if q == units[i]["quarters"] - 1:
                        evacuate(i, 2 * p)
                        evacuate(i, 2 * p + 1)
                elif kind == "columns":
                    dve.wait_ge(product, at("rows_turned"))
                    dve.tensor_copy(colT[:], ps[:, bank_of.get("cols", 0), 0:N_COLS])\
                        .then_inc(dve_result, mark(dve_result, "cols", ("free", "cols")))
                    dve.wait_ge(dve_result, now(dve_result))
                elif kind == "constants":
                    dve.wait_ge(late_loaded, at("late consts"))
                    dve.tensor_copy(cb[:], cb32).then_inc(dve_result, mark(dve_result, "masks"))
                    dve.wait_ge(dve_result, now(dve_result))
                    dve.memset(maskb[:, 0:P], 0.0).then_inc(dve_result, mark(dve_result))
                    dve.wait_ge(dve_result, now(dve_result))
                    dve.memset(maskb[0:64, 64:P], NEG).then_inc(dve_result, mark(dve_result))
                    dve.wait_ge(dve_result, now(dve_result))
                    for l in range(DEPTH):
                        note(("mask", l, 0), dve_result)
                        for j in range(2):
                            k = 4 * l + 2 * j
                            dve.tensor_tensor(lqk[:, k], lqk[:, k], lqk[:, k + 1], ALU.mult).then_inc(dve_result, mark(dve_result))
                            dve.wait_ge(dve_result, now(dve_result))
                            dve.tensor_reduce(lam[:, 2 * l + j:2 * l + j + 1], lqk[:, k], AX, ALU.add)\
                                .then_inc(dve_result, mark(dve_result, *(["lambda_sums"] if (l, j) == (1, 1) else [])))
                            dve.wait_ge(dve_result, now(dve_result))
                    dve.wait_ge(product, at("late_rows_turned"))
                    dve.tensor_copy(peT[:], ps[:, bank_of.get("late cols", 0), 128:192]).then_inc(dve_result, mark(dve_result))
                    dve.wait_ge(dve_result, now(dve_result))
                    dve.tensor_copy(modT[:, :, :], ps[:, bank_of.get("late cols", 0), 256:352].rearrange("p (l k) -> p l k", l=DEPTH))\
                        .then_inc(dve_result, mark(dve_result, ("free", "late cols")))
                    dve.wait_ge(dve_result, now(dve_result))
                    if 2 in blocks:
                        dve.wait_ge(act_result, at("c_tanh"))
                        dve.scalar_tensor_tensor(cact[:, 0:8], cact[:, 8:16], 1.0, col("c", 0, 0, 8), ALU.add, ALU.mult)\
                            .then_inc(dve_result, mark(dve_result))
                        dve.wait_ge(dve_result, now(dve_result))
                        dve.tensor_scalar(cact[:, 0:8], cact[:, 0:8], 0.5, None, ALU.mult).then_inc(dve_result, mark(dve_result))
                        dve.wait_ge(dve_result, now(dve_result))
                    dve.wait_ge(act_result, at("lambda_exps"))
                    for l in range(DEPTH):
                        init = 0.8 - 0.6 * float(np.exp(-0.3 * l))
                        dve.scalar_tensor_tensor(lam[:, l:l + 1], lam[:, 5 + 2 * l:6 + 2 * l], -init,
                                                 lam[:, 4 + 2 * l:5 + 2 * l], ALU.add, ALU.subtract)\
                            .then_inc(dve_result, mark(dve_result))
                        dve.wait_ge(dve_result, now(dve_result))
                elif kind == "stats":
                    _, stage, t = step
                    dve.wait_ge(act_result, at("ss", stage, t))
                    dve.tensor_scalar(nsm[:, 0, 0:1], stat[:, 7, t:t + 1], 1.0 / D, EPS, ALU.mult, ALU.add)\
                        .then_inc(dve_result, mark(dve_result))
                    dve.wait_ge(dve_result, now(dve_result))
                    rsqrt(nsm[:, 1, 0:1], nsm[:, 0, 0:1])
                    dve.tensor_scalar(xn[:, t % 2], xm[:, t], nsm[:, 1, 0:1], None, ALU.mult)\
                        .then_inc(dve_result, mark(dve_result, ("xn", stage, t)))
                elif kind == "turn":
                    _, stage, t = step
                    for hb in range(2):
                        key = ("scr", step, hb)
                        dve.wait_ge(product, at("turned", step, hb))
                        if scr_prev[key] is not None:
                            dve.wait_ge(*place("free", scr_prev[key]))
                        h32 = scr[:, scr_slot[key]].rearrange("p (c n) -> p c n", c=4)
                        src = ps[:, bank_of.get((step, hb), 0)].rearrange("p (c n) -> p c n", c=4)
                        if stage[0] == "n":
                            g = col("norm_g", stage[1], 4 * hb, 4).unsqueeze(2).to_broadcast([P, 4, P])
                            dve.tensor_tensor(h32, src, g, ALU.mult)\
                                .then_inc(dve_result, mark(dve_result, ("h32", step, hb), ("free", (step, hb))))
                            dve.wait_ge(dve_result, now(dve_result))
                        else:
                            lo = (0 if stage[0] == "a" else 24) + 4 * hb
                            g = gain[:, 0 if stage[0] == "a" else 1, 4 * hb:4 * hb + 4].unsqueeze(2).to_broadcast([P, 4, P])
                            shift = modT[:, stage[1], lo:lo + 4].unsqueeze(2).to_broadcast([P, 4, P])
                            dve.tensor_tensor(h32, src, g, ALU.mult)\
                                .then_inc(dve_result, mark(dve_result, ("free", (step, hb))))
                            dve.wait_ge(dve_result, now(dve_result))
                            dve.tensor_tensor(h32, h32, shift, ALU.add)\
                                .then_inc(dve_result, mark(dve_result, ("h32", step, hb)))
                            dve.wait_ge(dve_result, now(dve_result))
                        dve.wait_ge(act_result, at("hh", step, hb))
                        tile = slice(t * P, (t + 1) * P)
                        dve.tensor_tensor(hTl[:, 4 * hb:4 * hb + 4, tile], h32,
                                          hTh[:, 4 * hb:4 * hb + 4, tile].bitcast(F32), ALU.subtract)\
                            .then_inc(dve_result, mark(dve_result, ("h", stage, t, hb), ("free", key)))
                elif kind == "rstd":
                    _, l, name = step
                    nh = 4 if name[0] == "b" else 8
                    s = stat[:, SS[name], 0:4 * nh]
                    v = nsm[:, 0, 0:4 * nh]
                    dve.wait_ge(dve_result, at("sumsq", l, name, TILES - 1))
                    if name[0] == "e":
                        nh = {"ek": 4, "eq": 8}[name]
                        s, v = stat[:, SS[name], 0:4 * nh], nsm[:, 0, 0:4 * nh]
                        dve.tensor_scalar(v, s, 1.0 / 64, EPS, ALU.mult, ALU.add).then_inc(dve_result, mark(dve_result))
                        dve.wait_ge(dve_result, now(dve_result))
                        rsqrt(s, v)
                        continue
                    if name == "bq":
                        dve.memset(gaT[0:32, :], 1.0).then_inc(dve_result, mark(dve_result, ("ones_row", l)))
                        dve.wait_ge(dve_result, now(dve_result))
                    dve.tensor_scalar(v, s, nh / 512.0, EPS, ALU.mult, ALU.add).then_inc(dve_result, mark(dve_result))
                    dve.wait_ge(dve_result, now(dve_result))
                    if name[1] == "q":
                        rsqrt(nsm[:, 1, 0:4 * nh], v)
                        dve.tensor_scalar(s, nsm[:, 1, 0:4 * nh], float(nh / 512.0) ** 0.5, None, ALU.mult)\
                            .then_inc(dve_result, mark(dve_result, ("rstd", l, name)))
                        dve.wait_ge(dve_result, now(dve_result))
                    else:
                        rsqrt(s, v)
                elif kind == "key_turn":
                    _, l, name, t = step
                    nh = 4 if name[0] == "b" else 8
                    dve.wait_ge(act_result, at("ktok", l, name[0], t))
                    kv = ktok[:, t].rearrange("p (h d) -> p h d", h=nh)
                    r = stat[:, SS[name], t * nh:(t + 1) * nh].unsqueeze(2).to_broadcast([P, nh, 512 // nh])
                    dve.tensor_tensor(kv, kv, r, ALU.mult).then_inc(dve_result, mark(dve_result, ("scaled_key", l, name, t)))
                elif kind == "index":
                    _, l, t, h = step
                    key = ("scr", step)
                    W = WIDTH[t]
                    dve.wait_ge(act_result, at("relu", step))
                    r = scr[:, scr_slot[key], 0:W]
                    s = score[:, AT[t]:AT[t] + W]
                    w = smtok[:, t, P + 16 + h:P + 17 + h]
                    if h == 0:
                        dve.tensor_scalar(s, r, w, None, ALU.mult).then_inc(dve_result, mark(dve_result, ("free", key)))
                        dve.wait_ge(dve_result, now(dve_result))
                    else:
                        dve.scalar_tensor_tensor(s, r, w, s, ALU.mult, ALU.add)\
                            .then_inc(dve_result, mark(dve_result, ("free", key)))
                        dve.wait_ge(dve_result, now(dve_result))
                    if h == IDX_HEADS - 1:
                        dve.memset(score[0:64, AT[t] + W - 64:AT[t] + W], UNSEEN).then_inc(dve_result, mark(dve_result))
                        dve.wait_ge(dve_result, now(dve_result))
                elif kind == "topk":
                    _, l, t, r = step
                    s = score[:, AT[t]:AT[t] + WIDTH[t]]
                    dve.max(top8[:], s).then_inc(dve_result, mark(dve_result))
                    dve.wait_ge(dve_result, now(dve_result))
                    dve.match_replace(s, top8[:], s, TAKEN).then_inc(dve_result, mark(dve_result))
                    dve.wait_ge(dve_result, now(dve_result))
                    if r == TOPK // 8 - 1:
                        if l > 0:
                            dve.wait_ge(product, at("out", l - 1, "b", TILES - 1))
                        dve.tensor_scalar(maskb[:, AT[t]:AT[t] + WIDTH[t]], s, 0.67 * TAKEN, NEG, ALU.is_gt, ALU.mult)\
                            .then_inc(dve_result, mark(dve_result, ("mask", l, t)))
                        dve.wait_ge(dve_result, now(dve_result))
                elif kind == "decay1":
                    _, l, t = step
                    dve.wait_ge(product, at("rates", l, t))
                    dve.wait_ge(act_result, at("abs", l, t))
                    dve.tensor_scalar(mn[:, t], ps[:, bank_of.get(step, 0), 0:256], 0.0, None, ALU.min)\
                        .then_inc(dve_result, mark(dve_result, ("min", l, t), ("free", step)))
                elif kind == "decay2":
                    _, l = step
                    dve.wait_ge(act_result, at("ln", l))
                    dve.wait_ge(dve_result, at("min", l, TILES - 1))
                    dve.tensor_tensor(loga[:, :, :], mn[:, :, :], loga[:, :, :], ALU.subtract)\
                        .then_inc(dve_result, mark(dve_result, ("loga", l)))
                elif kind == "decay3":
                    _, l, t = step
                    dve.wait_ge(act_result, at("decays", l, t))
                    dve.wait_ge(act_result, at("gk", l, t))
                    dve.tensor_tensor(gk[:, t], gk[:, t], mn[:, t], ALU.mult).then_inc(dve_result, mark(dve_result, ("decayed_key", l, t)))
                elif kind == "state":
                    _, l, t = step
                    for cc in range(2):
                        dve.wait_ge(product, at("update", l, t, cc))
                        dve.wait_ge(act_result, at("decays", l, t))
                        b = ps[:, bank_of.get((step, cc), 0)]
                        n = 2 * t + cc
                        for pr in range(2):
                            for hh in range(2):
                                r = slice(64 * hh, 64 * hh + 64)
                                new = b[r, pr * 256 + hh * P:pr * 256 + (hh + 1) * P]
                                if n == 0:
                                    ins = dve.tensor_copy(S[r, pr, n], new)
                                else:
                                    ins = dve.scalar_tensor_tensor(S[r, pr, n], S[r, pr, n - 1], dec[r, pr, n:n + 1], new,
                                                                   ALU.mult, ALU.add)
                                if pr == 1 and hh == 1:
                                    ins\
                                        .then_inc(dve_result, mark(dve_result, ("free", (step, cc)), *([("states", l, t)] if cc else [])))
                                    dve.wait_ge(dve_result, now(dve_result))
                                else:
                                    ins.then_inc(dve_result, mark(dve_result))
                elif kind == "y_tok":
                    _, l, m, t = step
                    dve.wait_ge(product, at("out", l, m, t))
                    dve.wait_ge(dve_result, at("z", l, m, t))
                    y = y_at(l, m, t)
                    y3 = y.rearrange("p (h d) -> p h d", h=4)
                    if m != "b":
                        dve.wait_ge(act_result, at("osq", step))
                        dve.tensor_reduce(nsm[:, 0, 0:4], y3, AX, ALU.add).then_inc(dve_result, mark(dve_result))
                        dve.wait_ge(dve_result, now(dve_result))
                        dve.tensor_scalar(nsm[:, 0, 0:4], nsm[:, 0, 0:4], 1.0 / P, EPS, ALU.mult, ALU.add)\
                            .then_inc(dve_result, mark(dve_result))
                        dve.wait_ge(dve_result, now(dve_result))
                        rsqrt(nsm[:, 1, 0:4], nsm[:, 0, 0:4])
                        scale = 0.5 if m == "a" else 0.5 * (0.2 + 0.6 * float(np.exp(-0.3 * l)))
                        dve.tensor_scalar(nsm[:, 1, 0:4], nsm[:, 1, 0:4], scale, None, ALU.mult)\
                            .then_inc(dve_result, mark(dve_result))
                        dve.wait_ge(dve_result, now(dve_result))
                    for key in y_free(step):
                        dve.wait_ge(*place(key))
                    for n, (part, b, z) in enumerate(y_parts(step)):
                        key = ("free", (("gla_out", l, t), n) if m == "a" else ("value", l, m, t))
                        dve.tensor_tensor(part, b, z, ALU.mult)\
                            .then_inc(dve_result, mark(dve_result, key, *([("y_tok", l, m, t)] if m == "b" else [])))
                        dve.wait_ge(dve_result, now(dve_result))
                    if m != "b":
                        r = nsm[:, 1, 0:4].unsqueeze(2).to_broadcast([P, 4, P])
                        dve.tensor_tensor(y3, y3, r, ALU.mult)\
                            .then_inc(dve_result, mark(dve_result, *([("y_tok", l, m, t)] if m == "c" else [])))
                        dve.wait_ge(dve_result, now(dve_result))
                    if m == "a":
                        g = glag[:, l].unsqueeze(1).to_broadcast([P, 4, P])
                        dve.tensor_tensor(y3, y3, g, ALU.mult).then_inc(dve_result, mark(dve_result, ("y_tok", l, m, t)))
                        dve.wait_ge(dve_result, now(dve_result))
                elif kind == "y_turn":
                    _, l, m, t = step
                    dve.wait_ge(act_result, at("yh", step))
                    tile = slice(t * P, (t + 1) * P)
                    dve.tensor_tensor(yTl[:, :, tile], ps[:, bank_of.get(step, 0)].rearrange("p (c n) -> p c n", c=4),
                                      yTh[:, :, tile].bitcast(F32), ALU.subtract)\
                        .then_inc(dve_result, mark(dve_result, ("y", l, m, t), ("free", step)))
                elif kind == "logits":
                    _, l, m, t, h, c = step
                    s = soft[:, seq_of[step] % 8]
                    dve.wait_ge(product, at("logits", step))
                    dve.wait_ge(dve_result, at("rstd", l, m + "q"))
                    dve.reduce_max(s[:, 0:1], ps[:, bank_of.get(step, 0), 0:WIDTH[t]], AX)\
                        .then_inc(dve_result, mark(dve_result))
                    dve.wait_ge(dve_result, now(dve_result))
                    dve.tensor_scalar(s[:, 1:2], s[:, 0:1], q_scale(m, t, h, c), -1.0, ALU.mult, ALU.mult)\
                        .then_inc(dve_result, mark(dve_result, ("bias", step)))
                elif kind == "prob":
                    _, l, m, t, h = step
                    W = WIDTH[t]
                    parts = [("logits", l, m, t, h, c) for c in range(1 if m == "b" else 2)]
                    ss = [soft[:, seq_of[x] % 8] for x in parts]
                    pp = [PR[m][:, seq_of[x] % len_P[m], 0:W] for x in parts]
                    for x in parts:
                        dve.wait_ge(act_result, at("exp", x))
                    for s in ss:
                        dve.reciprocal(s[:, 3:4], s[:, 2:3]).then_inc(dve_result, mark(dve_result))
                        dve.wait_ge(dve_result, now(dve_result))
                    if m == "b":
                        dve.tensor_scalar(pp[0], pp[0], ss[0][:, 3:4], 0.5, ALU.mult, ALU.mult)\
                            .then_inc(dve_result, mark(dve_result, ("prob", step)))
                    else:
                        dve.tensor_scalar(pp[1], pp[1], ss[1][:, 3:4], lam[:, l:l + 1], ALU.mult, ALU.mult)\
                            .then_inc(dve_result, mark(dve_result))
                        dve.wait_ge(dve_result, now(dve_result))
                        dve.scalar_tensor_tensor(pp[0], pp[0], ss[0][:, 3:4], pp[1], ALU.mult, ALU.add)\
                            .then_inc(dve_result, mark(dve_result, ("prob", step)))
                    n = 4 * t + h
                    if n % 2 == 1:
                        dve.wait_ge(product, at("turned", step))
                        if n >= 2:
                            dve.wait_ge(product, at("value", l, m, n - 2))
                        dve.tensor_copy(PT[m][:, n % 2, 0:W], ps[:, bank_of.get(step, 0), 0:W])\
                            .then_inc(dve_result, mark(dve_result, ("PT", l, m, n), ("free", step)))
                elif kind == "mod":
                    m = step[1]
                    pair, j = m % 4, m // 4
                    acc = macc[:, j % 2]
                    dve.wait_ge(mod_loaded, at("modw", m))
                    if pair == 0 and j >= 2:
                        dve.wait_ge(product, at("mod_sum", j - 2))
                    for c in range(2):
                        k = 2 * pair + c
                        if k == 0:
                            dve.tensor_scalar(acc, modw[:, c], cact[:, k:k + 1], None, ALU.mult)\
                                .then_inc(dve_result, mark(dve_result))
                            dve.wait_ge(dve_result, now(dve_result))
                        else:
                            dve.scalar_tensor_tensor(acc, modw[:, c], cact[:, k:k + 1], acc, ALU.mult, ALU.add)\
                                .then_inc(dve_result, mark(dve_result, *([("mod", m)] if c else [])))
                            dve.wait_ge(dve_result, now(dve_result))
                elif kind == "mod_sum":
                    j = step[1]
                    dve.wait_ge(product, at("mod_sum", j))
                    two = modT[:, j // 24, 2 * (j % 24):2 * (j % 24) + 2]
                    dve.tensor_tensor(two, two, ps[:, bank_of.get(step, 0), 0:2], ALU.add)\
                        .then_inc(dve_result, mark(dve_result, ("free", step), *([("modT", j // 24)] if j % 24 == 23 else [])))
                    dve.wait_ge(dve_result, now(dve_result))
                elif kind == "gains":
                    l = step[1]
                    for j, (name, lo) in enumerate((("norm1", 8), ("norm2", 32))):
                        dve.scalar_tensor_tensor(gain[:, j], modT[:, l, lo:lo + 8], 1.0, col(name, l, 0, 8),
                                                 ALU.add, ALU.mult).then_inc(dve_result, mark(dve_result))
                        dve.wait_ge(dve_result, now(dve_result))
                elif kind in ("k_rope", "q_rope"):
                    _, l, t = step
                    key = ("scr", step)
                    name, nh = ("ek", 4) if kind == "k_rope" else ("eq", 8)
                    x = (ktk if name == "ek" else qtk)[:, t, 0:64 * nh]
                    x3 = x.rearrange("p (h d) -> p h d", h=nh)
                    dve.wait_ge(*place(("ktk", l, t) if name == "ek" else ("qtk", l, t)))
                    dve.wait_ge(vec_loaded, at("rope_loaded", l))
                    r = stat[:, SS[name], t * nh:(t + 1) * nh].unsqueeze(2).to_broadcast([P, nh, 64])
                    dve.tensor_tensor(x3, x3, r, ALU.mult).then_inc(dve_result, mark(dve_result))
                    dve.wait_ge(dve_result, now(dve_result))
                    if name == "eq":
                        dve.tensor_tensor(x3, x3, hgain[:, 0].unsqueeze(1).to_broadcast([P, 8, 64]), ALU.mult)\
                            .then_inc(dve_result, mark(dve_result))
                        dve.wait_ge(dve_result, now(dve_result))
                    else:
                        x4 = x.rearrange("p (b g d) -> p b g d", b=2, g=2)
                        g = hgain[:, 1:3].unsqueeze(2).to_broadcast([P, 2, 2, 64])
                        dve.tensor_tensor(x4, x4, g, ALU.mult).then_inc(dve_result, mark(dve_result))
                        dve.wait_ge(dve_result, now(dve_result))
                    if scr_prev[key] is not None:
                        dve.wait_ge(*place("free", scr_prev[key]))
                    tmp = scr[:, scr_slot[key], 0:64 * nh].rearrange("p (h d) -> p h d", h=nh)
                    rotate(x3, tmp, rot[:, t], nh)
                    prev = ("turned", (kind, l, t - 2)) if t >= 2 else ("turned", ("k_rope", l, t + 2)) if name == "eq" else None
                    if prev:
                        dve.wait_ge(*place(prev))
                    if name == "eq":
                        dve.tensor_tensor(tokr[:, t % 2].rearrange("p (h d) -> p h d", h=8), x3, tmp, ALU.add)\
                            .then_inc(dve_result, mark(dve_result, ("roped_q", l, t), ("free", key)))
                        dve.wait_ge(dve_result, now(dve_result))
                    else:
                        for half in range(2):
                            dst = tokr[:, t % 2].rearrange("p (h r d) -> p h r d", h=4, r=2)[:, :, half]
                            dve.tensor_tensor(dst, x3, tmp, ALU.add)\
                                .then_inc(dve_result, mark(dve_result, *([("roped_k", l, t), ("free", key)] if half else [])))
                            dve.wait_ge(dve_result, now(dve_result))
                elif kind == "cmp_in":
                    _, l, kv = step
                    dve.wait_ge(act_result, at("cT", l, TILES - 1))
                    src = cT[:, 2 * kv:2 * kv + 2, 0:496].rearrange("p g (n s) -> p s g n", s=16)
                    j = 16 * (2 * l + kv)
                    for g in range(2):
                        pe_ = peT[:, j:j + 16].unsqueeze(2).to_broadcast([P, 16, 31])
                        dve.tensor_tensor(cX[:, kv, :, g], src[:, :, g], pe_, ALU.add)\
                            .then_inc(dve_result, mark(dve_result, *([("cX", l, kv)] if g else [])))
                        dve.wait_ge(dve_result, now(dve_result))
                    if kv == 1:
                        dve.memset(small4[:, :], 0.0).then_inc(dve_result, mark(dve_result, ("sil_cleared", l)))
                        dve.wait_ge(dve_result, now(dve_result))
                        dve.memset(V4[:, :, :], 0.0).then_inc(dve_result, mark(dve_result, ("V4_cleared", l)))
                        dve.wait_ge(dve_result, now(dve_result))
                elif kind == "cmp_hidden":
                    _, l, kv = step
                    dve.wait_ge(act_result, at("hidden_tanh", l, kv))
                    b = ps[0:64, bank_of.get(step, 0)]
                    for g in range(2):
                        th, hid = chid[0:64, kv, 31 * g:31 * g + 31], b[:, 31 * g:31 * g + 31]
                        keys = [("free", step), ("silk" if kv == 0 else "silv", l)] if g else []
                        if kv == 0:
                            dve.scalar_tensor_tensor(silk[0:64, 32 * g:32 * g + 31], th, 1.0, hid, ALU.add, ALU.mult)\
                                .then_inc(dve_result, mark(dve_result, *keys))
                            dve.wait_ge(dve_result, now(dve_result))
                        else:
                            dst = silv[0:64, P * g:P * g + P].rearrange("p (r n) -> p r n", r=4)[:, :, 0:31]
                            dve.scalar_tensor_tensor(dst, th.unsqueeze(1).to_broadcast([64, 4, 31]), 1.0,
                                                     hid.unsqueeze(1).to_broadcast([64, 4, 31]), ALU.add, ALU.mult)\
                                .then_inc(dve_result, mark(dve_result, *keys))
                            dve.wait_ge(dve_result, now(dve_result))
                elif kind == "cmp_key":
                    _, l = step
                    key = ("scr", step)
                    dve.wait_ge(act_result, at("kc_raw", l))
                    dve.wait_ge(vec_loaded, at("rope_loaded", l))
                    if scr_prev[key] is not None:
                        dve.wait_ge(*place("free", scr_prev[key]))
                    x3 = kcd[0:32, 0:128].rearrange("p (g d) -> p g d", g=2)
                    tmp = scr[0:32, scr_slot[key], 0:128].rearrange("p (g d) -> p g d", g=2)
                    dve.tensor_tensor(tmp, x3, x3, ALU.mult).then_inc(dve_result, mark(dve_result))
                    dve.wait_ge(dve_result, now(dve_result))
                    v, r = nsm[0:32, 0, 0:2], nsm[0:32, 1, 0:2]
                    dve.tensor_reduce(v, tmp, AX, ALU.add).then_inc(dve_result, mark(dve_result))
                    dve.wait_ge(dve_result, now(dve_result))
                    dve.tensor_scalar(v, v, 1.0 / 64, EPS, ALU.mult, ALU.add).then_inc(dve_result, mark(dve_result))
                    dve.wait_ge(dve_result, now(dve_result))
                    rsqrt(r, v)
                    dve.tensor_tensor(x3, x3, r.unsqueeze(2).to_broadcast([32, 2, 64]), ALU.mult)\
                        .then_inc(dve_result, mark(dve_result))
                    dve.wait_ge(dve_result, now(dve_result))
                    dve.tensor_tensor(x3, x3, hgain[0:32, 3].unsqueeze(1).to_broadcast([32, 2, 64]), ALU.mult)\
                        .then_inc(dve_result, mark(dve_result))
                    dve.wait_ge(dve_result, now(dve_result))
                    rotate(x3, tmp, cmprot[0:32], 2, 32)
                    dve.tensor_tensor(tmp, x3, tmp, ALU.add).then_inc(dve_result, mark(dve_result, ("free", key)))
                    dve.wait_ge(dve_result, now(dve_result))
                    for half in range(2):
                        dst = kcd[0:32, :].rearrange("p (g r d) -> p g r d", g=2, r=2)[:, :, half]
                        dve.tensor_copy(dst, tmp)\
                            .then_inc(dve_result, mark(dve_result, *([("kc_roped", l)] if half else [])))
                        dve.wait_ge(dve_result, now(dve_result))
                elif kind == "pool":
                    _, l, g = step
                    keys = [("scr", step, 0), ("scr", step, 1)]
                    A = [scr[:, scr_slot[k]] for k in keys]
                    for k in keys:
                        if scr_prev[k] is not None:
                            dve.wait_ge(*place("free", scr_prev[k]))
                    dve.wait_ge(act_result, at("uT", l, g))
                    u, src = uT[:, g], uT[:, g]
                    order = [A[(g + j) % 2] for j in range(g + 1)]
                    order = order[::-1]
                    for j, dst in enumerate(order):
                        sh = 1 << j
                        dve.tensor_copy(dst[:, 0:sh], src[:, 0:sh]).then_inc(dve_result, mark(dve_result))
                        dve.wait_ge(dve_result, now(dve_result))
                        dve.tensor_tensor(dst[:, sh:T], src[:, sh:T], src[:, 0:T - sh], ALU.add)\
                            .then_inc(dve_result, mark(dve_result))
                        dve.wait_ge(dve_result, now(dve_result))
                        src = dst
                    other = A[0] if order[-1] is A[1] else A[1]
                    fin = A[0]
                    dve.tensor_tensor(other[:, 0:16], src[:, 0:16], edge[:, g], ALU.mult)\
                        .then_inc(dve_result, mark(dve_result))
                    dve.wait_ge(dve_result, now(dve_result))
                    dve.tensor_tensor(other[:, 0:16], other[:, 0:16], u[:, 0:16], ALU.subtract)\
                        .then_inc(dve_result, mark(dve_result))
                    dve.wait_ge(dve_result, now(dve_result))
                    dve.scalar_tensor_tensor(fin[:, 16:T], src[:, 16:T], 1.0 / (2 << g), u[:, 16:T], ALU.mult, ALU.subtract)\
                        .then_inc(dve_result, mark(dve_result))
                    dve.wait_ge(dve_result, now(dve_result))
                    if other is not fin:
                        dve.tensor_copy(fin[:, 0:16], other[:, 0:16]).then_inc(dve_result, mark(dve_result))
                        dve.wait_ge(dve_result, now(dve_result))
                    dve.memset(nsm[:, 2, 0:1], 0.0)\
                        .then_inc(dve_result, mark(dve_result, ("pooled_in", l, g), ("free", keys[1])))
                    dve.wait_ge(dve_result, now(dve_result))
                    dve.wait_ge(act_result, at("pool_high", l, g))
                    dve.scalar_tensor_tensor(hTl[:, g], ps[:, bank_of.get(step, 0)], col("pool_scale", l, g),
                                             hTh[:, g].bitcast(F32), ALU.mult, ALU.subtract)\
                        .then_inc(dve_result, mark(dve_result, ("pooled", l, g), ("free", step)))
                elif kind == "cmp_logits":
                    _, l, t = step
                    b0 = bank_of.get(step, 0)
                    dve.wait_ge(product, at("cmp_logits", l, t))
                    if t > 0:
                        dve.wait_ge(product, at("turned", ("cmp_turn2", l, t - 1)))
                    src = ps[:, b0:b0 + 2, 0:P].rearrange("p o (n k) -> p o n k", k=32)
                    mx = csoft[:, 0].rearrange("p (n o) -> p o n", o=2)
                    for odd in range(2):
                        dve.tensor_reduce(mx[:, odd], src[:, odd], AX, ALU.max).then_inc(dve_result, mark(dve_result))
                        dve.wait_ge(dve_result, now(dve_result))
                    dst = cS.rearrange("p (n o k) -> p o n k", o=2, k=32)
                    for odd in range(2):
                        dve.tensor_tensor(dst[:, odd], src[:, odd], mx[:, odd].unsqueeze(2).to_broadcast([P, 4, 32]),
                                          ALU.subtract)\
                            .then_inc(dve_result, mark(dve_result, *([("cmp_shifted", l, t), ("free", step)] if odd else [])))
                        dve.wait_ge(dve_result, now(dve_result))
                elif kind == "cmp_turn2":
                    pass
                elif kind == "pair_logits":
                    _, l, t, h = step
                    n, W, b0 = 8 * t + h, WIDTH[t], bank_of.get(step, 0)
                    s = soft2[:, n % 8]
                    dve.wait_ge(product, at("logits", step))
                    dve.tensor_reduce(s[:, 0:2], ps[:, b0:b0 + 2, 0:W], AX, ALU.max).then_inc(dve_result, mark(dve_result))
                    dve.wait_ge(dve_result, now(dve_result))
                    dve.tensor_scalar(s[:, 2:4], s[:, 0:2], -0.125, None, ALU.mult).then_inc(dve_result, mark(dve_result, ("bias", step)))
                elif kind == "pair_prob":
                    _, l, t, h = step
                    n, W, b0 = 8 * t + h, WIDTH[t], bank_of.get(step, 0)
                    s = soft2[:, n % 8]
                    if h == 0:
                        dve.wait_ge(act_result, at("cmp_exp", l, t))
                        c3 = cS.rearrange("p (h k) -> p h k", k=32)
                        dve.tensor_reduce(csoft[:, 1], c3, AX, ALU.add).then_inc(dve_result, mark(dve_result))
                        dve.wait_ge(dve_result, now(dve_result))
                        dve.reciprocal(csoft[:, 2], csoft[:, 1]).then_inc(dve_result, mark(dve_result))
                        dve.wait_ge(dve_result, now(dve_result))
                        dve.tensor_tensor(csoft[:, 3], csoft[:, 2], gts[:, t].rearrange("p (h b) -> p h b", b=3)[:, :, 0],
                                          ALU.mult).then_inc(dve_result, mark(dve_result))
                        dve.wait_ge(dve_result, now(dve_result))
                        dve.tensor_tensor(c3, c3, csoft[:, 3].unsqueeze(2).to_broadcast([P, 8, 32]), ALU.mult)\
                            .then_inc(dve_result, mark(dve_result, ("cmp_prob", l, t)))
                        dve.wait_ge(dve_result, now(dve_result))
                    dve.wait_ge(act_result, at("exp", ("pair_logits", l, t, h)))
                    dve.reciprocal(s[:, 6:8], s[:, 4:6]).then_inc(dve_result, mark(dve_result))
                    dve.wait_ge(dve_result, now(dve_result))
                    dve.tensor_tensor(s[:, 0:2], s[:, 6:8], gts[:, t, 3 * h + 1:3 * h + 3], ALU.mult)\
                        .then_inc(dve_result, mark(dve_result))
                    dve.wait_ge(dve_result, now(dve_result))
                    for j in range(2):
                        ins = dve.tensor_scalar(PP[:, n % 2, j, 0:W], PP[:, n % 2, j, 0:W], s[:, j:j + 1], None, ALU.mult)
                    ins.then_inc(dve_result, mark(dve_result, ("prob", step)))
                    if n % 2 == 1:
                        dve.wait_ge(product, at("turned", step))
                        if n >= 2:
                            dve.wait_ge(product, at("value2", l, n - 2))
                        dve.tensor_copy(PPT[:, n % 2, :, 0:W], ps[:, b0:b0 + 2, 0:W])\
                            .then_inc(dve_result, mark(dve_result, ("PPT", l, n), ("free", step)))
                elif kind == "o_turn":
                    _, l, t = step
                    dve.wait_ge(act_result, at("oh", l, t))
                    tile = slice(t * P, (t + 1) * P)
                    dve.tensor_tensor(hTl[:, 4:8, tile], ps[:, bank_of.get(step, 0)].rearrange("p (c n) -> p c n", c=4),
                                      hTh[:, 4:8, tile].bitcast(F32), ALU.subtract)\
                        .then_inc(dve_result, mark(dve_result, ("mo", l, t), ("free", step)))
                elif kind == "merge_turn":
                    _, l, t = step
                    tile = slice(t * P, (t + 1) * P)
                    for hb in range(2):
                        dve.wait_ge(act_result, at("mh", step, hb))
                        src = ps[:, bank_of.get((step, hb), 0)].rearrange("p (c n) -> p c n", c=4)
                        dve.scalar_tensor_tensor(hTl[:, 4 * hb:4 * hb + 4, tile], src, 0.5,
                                                 hTh[:, 4 * hb:4 * hb + 4, tile].bitcast(F32), ALU.mult, ALU.subtract)\
                            .then_inc(dve_result, mark(dve_result, ("m", l, t, hb), ("free", (step, hb))))
    return L


INPUTS = ["x", "norm_g", "w_in", "gla_wa2", "gla_ba", "gla_norm_g", "dsa_qn_g", "dsa_kn_g", "diff_qn_g", "diff_kn_g",
          "diff_lq1", "diff_lk1", "diff_lq2", "diff_lk2", "w_br", "w_out", "c_2", "w_mod_2", "b_mod_2", "norm1_2",
          "norm2_2", "w_in_2", "pool_w_2", "pool_scale_2", "q_norm_2", "k_norm_2", "cmp_pe_2", "cmp_w1_2", "cmp_w2_2",
          "w_out_2", "w_ff1_2", "w_ff2_2"]


def constants():
    cf = np.zeros((P, 452), np.float32)
    r = np.arange(P)
    cf[:, 0:128] = np.eye(P)
    cf[:, 128:256] = (r[:, None] > r[None, :]) & (r[:, None] // CHUNK == r[None, :] // CHUNK)
    cf[:, 256:258] = r[:, None] // CHUNK == np.arange(2)[None, :]
    cf[:, 258] = 1.0

    def rotation(pos):
        inv = np.float32(10000.0) ** (-np.arange(32, dtype=np.float32) * np.float32(2.0) / np.float32(64))
        ang = pos.astype(np.float32)[:, None] * inv[None, :].astype(np.float32)
        c, s = np.cos(ang), np.sin(ang)
        return np.concatenate([c, c, -s, s], axis=1).astype(np.float32)

    ends = np.arange(N_CMP) * CMP_STRIDE + CMP_LEN - 1
    cf[0:N_CMP, 259:387] = rotation(ends)
    for g in range(4):
        cf[:, 387 + 16 * g:387 + 16 * g + 16] = 1.0 / np.minimum(np.arange(16) + 1, 2 << g)
    cf[:, 451] = r >= CMP_LEN - 1
    cb = np.zeros((P, 512), np.float32)
    cb[:, 256:384] = np.where(r[None, :] > r[:, None], NEG, 0.0)
    for t in range(TILES):
        cb[:, 384 + 32 * t:384 + 32 * t + 31] = np.where(ends[None, :] > (t * P + r)[:, None], NEG, 0.0)
        cb[:, 384 + 32 * t + 31] = NEG
    cb[:, 0:128] = np.eye(P)
    cb[0:64, 192:256] = NEG
    return {"cf": cf, "cb": cb, "rot": rotation(np.arange(T))}


def program(draft, nc, arrays, result, **options):

    def tensors(nc):
        a = {n: nc.dram_tensor(f"in_{n}_dram", x.shape, mybir.dt.from_np(x.dtype), kind="ExternalInput").ap()
             for n, x in arrays.items()}
        a["x_kept"] = nc.dram_tensor("x_kept", (DEPTH, TILES, P, D), F32, kind="Internal").ap()
        return a, nc.dram_tensor("out_0_dram", result, F32, kind="ExternalOutput").ap()

    known = build(draft, *tensors(draft), **options)
    build(nc, *tensors(nc), known=known, **options)


def kernel(**inputs):
    import concourse.bacc as bacc
    from concourse.bass_utils import run_bass_kernel_spmd

    nc, draft = (bacc.Bacc("TRN2", target_bir_lowering=False, num_devices=1) for _ in range(2))
    arrays = {n: np.ascontiguousarray(inputs[n]) for n in INPUTS} | constants()
    program(draft, nc, arrays, arrays["x"].shape)
    r = run_bass_kernel_spmd(nc, [{f"in_{n}_dram": x for n, x in arrays.items()}], core_ids=[0])
    return r.results[0]["out_0_dram"]
```
